# Optimizing a Trainium2 kernel written in Bass

```python
import math
import jax, jax.numpy as jnp
from jax import lax
import numpy as np

D_MODEL = 2048
BATCH = 1
SEQ = 512
DEPTH = 1

N_MIXERS = 4
N_HEADS = 16
HEAD_DIM = D_MODEL // N_HEADS
MLA_HEADS = 16
MLA_Q_LORA = 512
MLA_KV_LORA = 512
MLA_NOPE = 128
MLA_ROPE = 64
MLA_V = 128
ROPE_THETA = 10000.0
HGRN_EXPAND = 128
HGRN_HEADS = D_MODEL // HGRN_EXPAND
HGRN_KDIM = HGRN_EXPAND
HGRN_VDIM = D_MODEL // HGRN_HEADS
HGRN_CHUNK = 64
Q_BLOCK = 128
MOBA_BLOCK = 256
MOBA_TOPK = 3
MOBA_Q_CHUNK = 16
D_FF = 4 * D_MODEL
ALPHA = float((2 * DEPTH) ** 0.25)
BETA = float((8 * DEPTH) ** -0.25)
LN_EPS = 1e-5
RMS_EPS = 1e-6
N_MLA_LAYERS = len(range(0, DEPTH, N_MIXERS))
N_HGRN_LAYERS = len(range(1, DEPTH, N_MIXERS))
N_SB_LAYERS = len(range(2, DEPTH, N_MIXERS))
N_MOBA_LAYERS = len(range(3, DEPTH, N_MIXERS))

kernel_name = "hybrid_mla_hgrn2_stickbreak_moba_deepnorm"

F32 = jnp.float32

def layer_norm(x, g, b):
    xf = x.astype(F32)
    mu = jnp.mean(xf, axis=-1, keepdims=True)
    var = jnp.mean(jnp.square(xf - mu), axis=-1, keepdims=True)
    y = (xf - mu) * lax.rsqrt(var + LN_EPS) * g.astype(F32) + b.astype(F32)
    return y.astype(x.dtype)

def rms_norm(x, g):
    xf = x.astype(F32)
    y = xf * lax.rsqrt(jnp.mean(jnp.square(xf), axis=-1, keepdims=True) + RMS_EPS) * g.astype(F32)
    return y.astype(x.dtype)

def rope_cos_sin(S):
    inv = 1.0 / (ROPE_THETA ** (jnp.arange(0, MLA_ROPE, 2, dtype=F32) / MLA_ROPE))
    ang = jnp.arange(S, dtype=F32)[:, None] * inv[None, :]
    return jnp.cos(ang), jnp.sin(ang)

def apply_rope(x, cos, sin):
    x1, x2 = x[..., : MLA_ROPE // 2], x[..., MLA_ROPE // 2:]
    y = jnp.concatenate([x1 * cos - x2 * sin, x2 * cos + x1 * sin], axis=-1)
    return y.astype(x.dtype)

def causal_softmax_attention(q, k, v, scale):
    B, H, S, dk = q.shape
    nq = S // Q_BLOCK
    qb = q.reshape(B, H, nq, Q_BLOCK, dk).transpose(2, 0, 1, 3, 4)
    key_pos = jnp.arange(S)

    def one_block(args):
        q_blk, i = args
        s = jnp.einsum('bhqd,bhkd->bhqk', q_blk, k).astype(F32) * scale
        q_pos = i * Q_BLOCK + jnp.arange(Q_BLOCK)
        s = jnp.where(key_pos[None, :] <= q_pos[:, None], s, -jnp.inf)
        p = jax.nn.softmax(s, axis=-1).astype(v.dtype)
        return jnp.einsum('bhqk,bhkd->bhqd', p, v)

    o = lax.map(one_block, (qb, jnp.arange(nq)))
    return o.transpose(1, 0, 3, 2, 4).reshape(B, S, H, v.shape[-1])

def mla_mixer(x, w_in, q_norm, kv_norm, w_uq, w_ukv, w_o):
    B, S, _ = x.shape
    h = x @ w_in
    cq = h[..., :MLA_Q_LORA]
    ckv = h[..., MLA_Q_LORA:MLA_Q_LORA + MLA_KV_LORA]
    k_rope = h[..., MLA_Q_LORA + MLA_KV_LORA:]
    cq = rms_norm(cq, q_norm)
    ckv = rms_norm(ckv, kv_norm)
    q = (cq @ w_uq).reshape(B, S, MLA_HEADS, MLA_NOPE + MLA_ROPE)
    kv = (ckv @ w_ukv).reshape(B, S, MLA_HEADS, MLA_NOPE + MLA_V)
    q_nope, q_rope = q[..., :MLA_NOPE], q[..., MLA_NOPE:]
    k_nope, v = kv[..., :MLA_NOPE], kv[..., MLA_NOPE:]
    cos, sin = rope_cos_sin(S)
    q_rope = apply_rope(q_rope, cos[:, None, :], sin[:, None, :])
    k_rope = apply_rope(k_rope, cos, sin)
    k_rope = jnp.broadcast_to(k_rope[:, :, None, :], (B, S, MLA_HEADS, MLA_ROPE))
    q = jnp.concatenate([q_nope, q_rope], axis=-1).transpose(0, 2, 1, 3)
    k = jnp.concatenate([k_nope, k_rope], axis=-1).transpose(0, 2, 1, 3)
    v = v.transpose(0, 2, 1, 3)
    o = causal_softmax_attention(q, k, v, (MLA_NOPE + MLA_ROPE) ** -0.5)
    return o.reshape(B, S, MLA_HEADS * MLA_V) @ w_o

def hgrn2_mixer(x, w_in, lb, o_norm, w_o):
    B, S, D = x.shape
    q, f_pre, i_in, g = jnp.split(x @ w_in, 4, axis=-1)
    lb = lb.astype(F32)
    log_f = jnp.logaddexp(jnp.log(lb), jnp.log1p(-lb) + jax.nn.log_sigmoid(f_pre.astype(F32)))
    k = -jnp.expm1(log_f)
    n = S // HGRN_CHUNK

    def chunks(t, dh):
        return t.astype(F32).reshape(B, n, HGRN_CHUNK, HGRN_HEADS, dh).transpose(1, 0, 3, 2, 4)

    xs = (chunks(q, HGRN_KDIM), chunks(k, HGRN_KDIM), chunks(i_in, HGRN_VDIM), chunks(log_f, HGRN_KDIM))
    causal = jnp.tril(jnp.ones((HGRN_CHUNK, HGRN_CHUNK), dtype=bool))

    def step(state, inp):
        qc, kc, vc, lf = inp
        b = jnp.cumsum(lf, axis=2)
        diff = b[:, :, :, None, :] - b[:, :, None, :, :]
        decay = jnp.exp(jnp.where(causal[:, :, None], diff, -jnp.inf))
        a = jnp.sum(qc[:, :, :, None, :] * kc[:, :, None, :, :] * decay, axis=-1)
        o = (jnp.einsum('bhts,bhsv->bhtv', a, vc)
             + jnp.einsum('bhtd,bhdv->bhtv', qc * jnp.exp(b), state))
        b_end = b[:, :, -1, :]
        state = (jnp.exp(b_end)[..., None] * state
                 + jnp.einsum('bhsd,bhsv->bhdv', kc * jnp.exp(b_end[:, :, None, :] - b), vc))
        return state, o

    state0 = jnp.zeros((B, HGRN_HEADS, HGRN_KDIM, HGRN_VDIM), F32)
    _, o = lax.scan(step, state0, xs)
    o = o.transpose(1, 0, 3, 2, 4).reshape(B, S, HGRN_HEADS, HGRN_VDIM)
    o = rms_norm(o, o_norm.reshape(HGRN_HEADS, HGRN_VDIM))
    o = o.reshape(B, S, D).astype(x.dtype) * jax.nn.silu(g)
    return o @ w_o

def stick_breaking_attention(q, k, v):
    B, H, S, d = q.shape
    scale = d ** -0.5
    nq = S // Q_BLOCK
    qb = q.reshape(B, H, nq, Q_BLOCK, d).transpose(2, 0, 1, 3, 4)
    key_pos = jnp.arange(S)

    def one_block(args):
        q_blk, i = args
        z = jnp.einsum('bhqd,bhkd->bhqk', q_blk, k).astype(F32) * scale
        q_pos = i * Q_BLOCK + jnp.arange(Q_BLOCK)
        strict = key_pos[None, :] < q_pos[:, None]
        log_1m = jnp.where(strict, jax.nn.log_sigmoid(-z), 0.0)
        after = lax.cumsum(log_1m, axis=3, reverse=True) - log_1m
        w = jnp.where(strict, jnp.exp(jax.nn.log_sigmoid(z) + after), 0.0).astype(v.dtype)
        return jnp.einsum('bhqk,bhkd->bhqd', w, v)

    o = lax.map(one_block, (qb, jnp.arange(nq)))
    return o.transpose(1, 0, 3, 2, 4).reshape(B, S, H, d)

def stick_breaking_mixer(x, w_in, w_o):
    B, S, D = x.shape
    q, k, v = jnp.split(x @ w_in, 3, axis=-1)
    heads = lambda t: t.reshape(B, S, N_HEADS, HEAD_DIM).transpose(0, 2, 1, 3)
    o = stick_breaking_attention(heads(q), heads(k), heads(v))
    return o.reshape(B, S, D) @ w_o

def moba_attention(q, k, v):
    B, H, S, d = q.shape
    s_pad = -(-S // MOBA_BLOCK) * MOBA_BLOCK
    pad = ((0, 0), (0, 0), (0, s_pad - S), (0, 0))
    q, k, v = jnp.pad(q, pad), jnp.pad(k, pad), jnp.pad(v, pad)
    nb = s_pad // MOBA_BLOCK
    k_sel = min(MOBA_TOPK, nb)
    scale = d ** -0.5
    k_blocks = k.reshape(B, H, nb, MOBA_BLOCK, d)
    v_blocks = v.reshape(B, H, nb, MOBA_BLOCK, d)
    k_mean = jnp.mean(k_blocks.astype(F32), axis=3)
    gate = jnp.einsum('bhsd,bhnd->bhsn', q.astype(F32), k_mean)
    q_blk = jnp.arange(s_pad) // MOBA_BLOCK
    fully_past = jnp.arange(nb)[None, :] < q_blk[:, None]
    gate = jnp.where(fully_past, gate, -jnp.inf)
    _, sel = lax.top_k(gate, k_sel)
    n_chunks = s_pad // MOBA_Q_CHUNK
    q_c = q.reshape(B, H, n_chunks, MOBA_Q_CHUNK, d).transpose(2, 0, 1, 3, 4)
    sel_c = sel.reshape(B, H, n_chunks, MOBA_Q_CHUNK, k_sel).transpose(2, 0, 1, 3, 4)
    b_idx = jnp.arange(B)[:, None, None, None]
    h_idx = jnp.arange(H)[None, :, None, None]
    n_g = k_sel * MOBA_BLOCK

    def one_chunk(args):
        qb, sb, ci = args
        start = ci * MOBA_Q_CHUNK
        blk = start // MOBA_BLOCK
        q_pos = start + jnp.arange(MOBA_Q_CHUNK)
        k_g = k_blocks[b_idx, h_idx, sb]
        v_g = v_blocks[b_idx, h_idx, sb]
        s_g = jnp.einsum('bhqd,bhqrkd->bhqrk', qb, k_g).astype(F32) * scale
        valid = jnp.arange(k_sel) < blk
        s_g = jnp.where(valid[None, None, None, :, None], s_g, -jnp.inf)
        k_own = lax.dynamic_slice_in_dim(k, blk * MOBA_BLOCK, MOBA_BLOCK, axis=2)
        v_own = lax.dynamic_slice_in_dim(v, blk * MOBA_BLOCK, MOBA_BLOCK, axis=2)
        s_own = jnp.einsum('bhqd,bhkd->bhqk', qb, k_own).astype(F32) * scale
        own_pos = blk * MOBA_BLOCK + jnp.arange(MOBA_BLOCK)
        s_own = jnp.where(own_pos[None, :] <= q_pos[:, None], s_own, -jnp.inf)
        logits = jnp.concatenate([s_g.reshape(B, H, MOBA_Q_CHUNK, n_g), s_own], axis=-1)
        p = jax.nn.softmax(logits, axis=-1).astype(v.dtype)
        p_g = p[..., :n_g].reshape(B, H, MOBA_Q_CHUNK, k_sel, MOBA_BLOCK)
        return (jnp.einsum('bhqrk,bhqrkd->bhqd', p_g, v_g)
                + jnp.einsum('bhqk,bhkd->bhqd', p[..., n_g:], v_own))

    o = lax.map(one_chunk, (q_c, sel_c, jnp.arange(n_chunks)))
    o = o.transpose(1, 0, 3, 2, 4).reshape(B, s_pad, H, d)
    return o[:, :S]

def moba_mixer(x, w_in, w_o):
    B, S, D = x.shape
    q, k, v = jnp.split(x @ w_in, 3, axis=-1)
    heads = lambda t: t.reshape(B, S, N_HEADS, HEAD_DIM).transpose(0, 2, 1, 3)
    o = moba_attention(heads(q), heads(k), heads(v))
    return o.reshape(B, S, D) @ w_o

def sq_relu_mlp(x, w1, w2):
    return jnp.square(jax.nn.relu(x @ w1)) @ w2

def setup_inputs(seed: int = 0) -> dict:
    key = jax.random.key(seed)
    ks = jax.random.split(key, 20)

    def dense(k, shape, fan_in, scale=1.0):
        return jax.random.normal(k, shape, F32) * (scale * fan_in ** -0.5)

    def gain(k, shape):
        return 1.0 + 0.05 * jax.random.normal(k, shape, F32)

    D = D_MODEL
    mla_in_w = MLA_Q_LORA + MLA_KV_LORA + MLA_ROPE
    return {
        "x": jax.random.normal(ks[0], (BATCH, SEQ, D), F32),
        "mla_w_in": dense(ks[1], (N_MLA_LAYERS, D, mla_in_w), D),
        "mla_q_norm": gain(ks[2], (N_MLA_LAYERS, MLA_Q_LORA)),
        "mla_kv_norm": gain(ks[3], (N_MLA_LAYERS, MLA_KV_LORA)),
        "mla_w_uq": dense(ks[4], (N_MLA_LAYERS, MLA_Q_LORA, MLA_HEADS * (MLA_NOPE + MLA_ROPE)), MLA_Q_LORA),
        "mla_w_ukv": dense(ks[5], (N_MLA_LAYERS, MLA_KV_LORA, MLA_HEADS * (MLA_NOPE + MLA_V)), MLA_KV_LORA),
        "mla_w_o": dense(ks[6], (N_MLA_LAYERS, MLA_HEADS * MLA_V, D), MLA_HEADS * MLA_V, BETA),
        "hgrn_w_in": dense(ks[7], (N_HGRN_LAYERS, D, 4 * D), D),
        "hgrn_lb_logits": 0.1 * jax.random.normal(ks[8], (DEPTH, D), F32),
        "hgrn_o_norm": gain(ks[9], (N_HGRN_LAYERS, D)),
        "hgrn_w_o": dense(ks[10], (N_HGRN_LAYERS, D, D), D, BETA),
        "sb_w_in": dense(ks[11], (N_SB_LAYERS, D, 3 * D), D),
        "sb_w_o": dense(ks[12], (N_SB_LAYERS, D, D), D, BETA),
        "moba_w_in": dense(ks[13], (N_MOBA_LAYERS, D, 3 * D), D),
        "moba_w_o": dense(ks[14], (N_MOBA_LAYERS, D, D), D, BETA),
        "ln_g": gain(ks[15], (DEPTH, 2, D)),
        "ln_b": 0.02 * jax.random.normal(ks[16], (DEPTH, 2, D), F32),
        "mlp_w1": dense(ks[17], (DEPTH, D, D_FF), D),
        "mlp_w2": dense(ks[18], (DEPTH, D_FF, D), D_FF, BETA),
    }

def reference(x, mla_w_in, mla_q_norm, mla_kv_norm, mla_w_uq, mla_w_ukv, mla_w_o,
              hgrn_w_in, hgrn_lb_logits, hgrn_o_norm, hgrn_w_o,
              sb_w_in, sb_w_o, moba_w_in, moba_w_o,
              ln_g, ln_b, mlp_w1, mlp_w2):
    lb_p = jax.nn.softmax(hgrn_lb_logits.astype(F32), axis=0)
    lower_bounds = jnp.cumsum(lb_p, axis=0) - lb_p[0]
    h = x
    for i in range(DEPTH):
        kind, slot = i % N_MIXERS, i // N_MIXERS
        if kind == 0:
            y = mla_mixer(h, mla_w_in[slot], mla_q_norm[slot], mla_kv_norm[slot],
                          mla_w_uq[slot], mla_w_ukv[slot], mla_w_o[slot])
        elif kind == 1:
            y = hgrn2_mixer(h, hgrn_w_in[slot], lower_bounds[i], hgrn_o_norm[slot], hgrn_w_o[slot])
        elif kind == 2:
            y = stick_breaking_mixer(h, sb_w_in[slot], sb_w_o[slot])
        else:
            y = moba_mixer(h, moba_w_in[slot], moba_w_o[slot])
        h = layer_norm(ALPHA * h + y, ln_g[i, 0], ln_b[i, 0])
        h = layer_norm(ALPHA * h + sq_relu_mlp(h, mlp_w1[i], mlp_w2[i]), ln_g[i, 1], ln_b[i, 1])
    return h


_drawn_inputs = setup_inputs


def setup_inputs(seed=0):
    import zlib

    import numpy as np

    out = dict(_drawn_inputs(seed))
    spreads = {}
    factors = {'mla_q_norm': 8.0, 'mla_kv_norm': 8.0}
    for name, (base, spread) in spreads.items():
        noise = np.random.default_rng([zlib.crc32(name.encode()), seed]).standard_normal(out[name].shape)
        drawn = base * np.exp(spread * noise) if base else spread * noise
        out[name] = __import__('jax').numpy.asarray(drawn.astype(out[name].dtype))
    for name, factor in factors.items():
        out[name] = (out[name] * factor).astype(out[name].dtype)
    return out
```

```python
import concourse.bass as bass
from concourse import mybir
from contextlib import ExitStack

P = 128
D = 2048
S = 512
KD = D // P
TT = S // P
LORA = 512
KL = LORA // P
HEADS = 16
PAIRS = HEADS // 2
NOPE, ROPE, VDIM = 128, 64, 128
FF = 4 * D
CHUNK = 8
CHUNKS = FF // P // CHUNK
CG = D // 512
ALPHA = 2.0 ** 0.25
SCALE = (NOPE + ROPE) ** -0.5
LN_EPS, RMS_EPS = 1e-5, 1e-6
MASKED = -1e30

HB = 1024
IN_TILES = 2 * KL + 1
IN_HB = 2 * IN_TILES
QKV_HB = 4
HB_QKV = IN_HB
HB_O = HB_QKV + QKV_HB * PAIRS
O_HB = CG * KD // 2
HB_MLP = HB_O + O_HB
UP_HB = 2 * CHUNK
DOWN_HB = CG * CHUNK // 2
MLP_HB = UP_HB + DOWN_HB
N_HB = HB_MLP + CHUNKS * MLP_HB
SLOTS = 4
RAWS = 2

SCORE_AT = {0: 0, 2: 128, 3: 512, 1: 1024}
PROB_T_AT = {0: 0, 1: 512, 3: 896, 2: 1024}
SCORE_COLS = 1280


def mla_mlp_program(nc, xT, x, w, const, gain, ln, out):
    f32, f32r = mybir.dt.float32, mybir.dt.float32r
    ALU, ACT, AX = mybir.AluOpType, mybir.ActivationFunctionType, mybir.AxisListType

    with ExitStack() as ctx:
        arena = ctx.enter_context(nc.sbuf_tensor("arena", [P, 53200], f32))
        base = nc.sbuf_base - 53200 * 4
        place = [base]

        def sb(name, shape, dt=f32, at=None):
            size = 4
            for n in shape[1:]:
                size *= n
            if at is None:
                at = place[0]
                place[0] += size
            assert at + size <= base + 53200 * 4, name
            return nc.alloc_sbuf_tensor_at(name, shape, dt, offset=at)

        def sem(name):
            return ctx.enter_context(nc.semaphore(name))

        act_hi, act_lo = sb("act_hi", [P, KD, S], f32r), sb("act_lo", [P, KD, S], f32r)
        mid_hi, mid_lo = sb("mid_hi", [P, 8, S], f32r), sb("mid_lo", [P, 8, S], f32r)
        raw = sb("raw", [P, RAWS, HB])
        w_hi, w_lo = sb("w_hi", [P, SLOTS, HB], f32r), sb("w_lo", [P, SLOTS, HB], f32r)
        table = sb("table", [P, 2 * P + 2 * S])
        ident = table[:, 0:P]
        mask = table[:, P:2 * P]
        rope_cos = table[:, 2 * P:2 * P + S]
        rope_sin = table[:, 2 * P + S:2 * P + 2 * S]
        two = table[:, 2 * P:2 * P + 2 * S].rearrange("p (a s) -> p a s", a=2)
        ident_r, mask_r = sb("ident_r", [P, P], f32r), sb("mask_r", [P, P], f32r)
        ones = sb("ones", [P, P])
        gains = sb("gains", [P, 8 + 2 * KD])
        small = sb("small", [P, 160])
        ssq, root, inv, tmp, rstd = (small[:, 4 * i:4 * i + 4] for i in range(5))
        nmr = small[:, 20:24]
        moments = small[:, 24:32].rearrange("p (t m) -> p t m", m=2)
        row_max = small[:, 32:40].rearrange("p (h t) -> p h t", h=2)
        neg_max = small[:, 40:48].rearrange("p (h t) -> p h t", h=2)
        row_sum = small[:, 48:56].rearrange("p (h t) -> p h t", h=2)
        inv_sum = small[:, 56:64].rearrange("p (h t) -> p h t", h=2)
        stats = small[:, 64:160].rearrange("p (t c s) -> p t c s", t=TT, c=CG)
        overlay = place[0]

        probs = sb("probs", [P, 2, SCORE_COLS])
        pt_hi = sb("pt_hi", [P, 2, SCORE_COLS], f32r)
        pt_lo = sb("pt_lo", [P, 2, SCORE_COLS], f32r)
        load_area = place[0]
        k_hi, k_lo = sb("k_hi", [P, 2, S], f32r), sb("k_lo", [P, 2, S], f32r)
        qr_hi, qr_lo = sb("qr_hi", [P, S], f32r), sb("qr_lo", [P, S], f32r)
        kr_hi, kr_lo = sb("kr_hi", [P, 2, S], f32r), sb("kr_lo", [P, 2, S], f32r)
        v_hi, v_lo = sb("v_hi", [P, TT, 2 * VDIM], f32r), sb("v_lo", [P, TT, 2 * VDIM], f32r)
        rot, swap = sb("rot", [P, S]), sb("swap", [P, S])
        q_hi, q_lo = act_hi[:, HEADS - 2:HEADS, :], act_lo[:, HEADS - 2:HEADS, :]
        x_raw = sb("x_raw", [P, KD, S], at=load_area)
        latent = sb("latent", [P, 2 * KL, S], at=overlay)
        square = sb("square", [P, KL, S], at=overlay + 4 * 2 * KL * S)
        diag = sb("diag", [P, TT, P], at=overlay + 4 * 3 * KL * S)
        rows = sb("rows", [P, TT, D], at=overlay)
        ln_rows = sb("ln_rows", [P, 4, D], at=overlay + 4 * TT * D)

        bank = ctx.enter_context(nc.psum_tensor("bank", [P, 8, 512], f32))

        def score_bank(h):
            return bank[:, 3 * h:3 * h + 3, :].rearrange("p b n -> p (b n)")

        x_loaded = [sem(f"x_loaded{i}") for i in range(KD // 2)]
        table_loaded, gains_loaded = sem("table_loaded"), sem("gains_loaded")
        rows_loaded = [sem(f"rows_loaded{t}") for t in range(TT)]
        ln_loaded = [sem(f"ln_loaded{i}") for i in range(4)]
        stored = [sem(f"stored{t}") for t in range(TT)]
        raw_loaded = [sem(f"raw_loaded{i}") for i in range(RAWS)]
        w_begun, w_hi_made, w_split, w_used = sem("w_begun"), sem("w_hi_made"), sem("w_split"), sem("w_used")
        x_hi_made, x_split = sem("x_hi_made"), sem("x_split")
        consts_made = sem("consts_made")
        in_done, latent_kept, squared = sem("in_done"), sem("latent_kept"), sem("squared")
        ssq_done, var_made, root_made, dve_chain = sem("ssq_done"), sem("var_made"), sem("root_made"), sem("dve_chain")
        diag_made, inv_spread = sem("diag_made"), sem("inv_spread")
        latent_scaled, latent_hi, latent_split = sem("latent_scaled"), sem("latent_hi"), sem("latent_split")
        rope_done, rope_swapped, rope_cosined = sem("rope_done"), sem("rope_swapped"), sem("rope_cosined")
        rope_sined, rope_rotated, rope_hi, rope_split = sem("rope_sined"), sem("rope_rotated"), sem("rope_hi"), sem("rope_split")
        zeroed = sem("zeroed")
        proj_done, proj_hi, proj_split = sem("proj_done"), sem("proj_hi"), sem("proj_split")
        scored, maxed, max_negated = sem("scored"), sem("maxed"), sem("max_negated")
        exped, sum_inverted, normed = sem("exped"), sem("sum_inverted"), sem("normed")
        transposed, pt_hi_made, pt_split = sem("transposed"), sem("pt_hi_made"), sem("pt_split")
        pv_done, o_hi_made, o_split = sem("pv_done"), sem("o_hi_made"), sem("o_split")
        block_done, rows_added, row_stats = sem("block_done"), sem("rows_added"), sem("row_stats")
        row_scaled, t_done, t_affine, t_hi, t_split = sem("row_scaled"), sem("t_done"), sem("t_affine"), sem("t_hi"), sem("t_split")
        residual_scaled, residual_made = sem("residual_scaled"), sem("residual_made")
        up_done, relu_made, hid_hi, hid_squared, hid_split = sem("up_done"), sem("relu_made"), sem("hid_hi"), sem("hid_squared"), sem("hid_split")
        out_gained, out_made = sem("out_gained"), sem("out_made")

        block = ctx.enter_context(nc.Block())

        @block.sync
        def _(sp):
            for n in range(RAWS):
                sp.dma_start(raw[:, n, :], w[n]).then_inc(raw_loaded[n], 16)
            with sp.Fori(1, N_HB // RAWS) as i:
                for s in range(RAWS):
                    sp.wait_ge(w_split, RAWS * i + s - RAWS + 1)
                    sp.dma_start(raw[:, s, :], w[bass.ds(RAWS * i + s, 1)].rearrange("o p n -> (o p) n"))\
                      .then_inc(raw_loaded[s], 16)
            for t in range(TT):
                sp.wait_ge(out_made, t + 1)
                sp.dma_start(out[t], rows[:, t, :]).then_inc(stored[t], 16)
            for t in range(TT):
                sp.wait_ge(stored[t], 16)

        @block.gpsimd
        def _(pool):
            def split(turn, s, ring_full):
                pool.wait_ge(raw_loaded[s % RAWS], 16 * (SLOTS // RAWS * turn + s // RAWS + 1))
                if ring_full:
                    pool.wait_ge(w_used, SLOTS * turn + s - SLOTS + 1)
                pool.sem_inc(w_begun, 1)
                pool.tensor_copy(w_hi[:, s, :], raw[:, s % RAWS, :]).then_inc(w_hi_made, 1)
                pool.wait_ge(w_hi_made, SLOTS * turn + s + 1)
                pool.tensor_tensor(w_lo[:, s, :], raw[:, s % RAWS, :], w_hi[:, s, :].bitcast(f32), ALU.subtract)\
                    .then_inc(w_split, 1)

            for s in range(SLOTS):
                split(0, s, False)
            with pool.Fori(1, N_HB // SLOTS) as turn:
                for s in range(SLOTS):
                    split(turn, s, True)
            for s in range(N_HB % SLOTS):
                split(N_HB // SLOTS, s, True)

        @block.scalar
        def _(act):
            for i in range(KD // 2):
                act.dma_start(x_raw[:, 2 * i:2 * i + 2, :], xT[:, 2 * i:2 * i + 2, :]).then_inc(x_loaded[i], 16)
            act.dma_start(table[:, :], const).then_inc(table_loaded, 16)
            act.dma_start(gains[:, :], gain).then_inc(gains_loaded, 16)
            for k in range(KD):
                act.wait_ge(x_loaded[k // 2], 16)
                act.activation(act_hi[:, k, :], x_raw[:, k, :], ACT.Copy).then_inc(x_hi_made, 1)
            act.wait_ge(table_loaded, 16)
            act.activation(ident_r[:, :], ident, ACT.Copy)
            act.activation(mask_r[:, :], mask, ACT.Copy).then_inc(consts_made, 1)

            def keep_latent(j):
                act.wait_ge(in_done, j + 1)
                if j == KL:
                    act.wait_ge(ssq_done, 1)
                act.activation(latent[:, j, :], bank[:, j % 2, :], ACT.Copy)
                act.activation(square[:, j % KL, :], bank[:, j % 2, :], ACT.Square).then_inc(latent_kept, 1)

            def root_of(n):
                act.wait_ge(var_made, n + 1)
                act.activation(root, ssq, ACT.Sqrt).then_inc(root_made, 1)

            def latent_his(g):
                for j in range(KL * g, KL * g + KL):
                    act.wait_ge(latent_scaled, j + 1)
                    act.activation(mid_hi[:, j, :], latent[:, j, :], ACT.Copy).then_inc(latent_hi, 1)

            def rope_swap(r):
                act.wait_ge(rope_done, r + 1)
                if r is not KEY:
                    act.wait_ge(rope_rotated, r)
                for q in range(4):
                    last = act.activation(swap[32 * q:32 * q + 32, :],
                                          bank[32 * (q ^ 1):32 * (q ^ 1) + 32, 0 if r is KEY else 6, :], ACT.Copy)
                last.then_inc(rope_swapped, 1)

            KEY = 0
            for j in range(KL):
                keep_latent(j)
            for j in range(KL, 6):
                keep_latent(j)
            root_of(0)
            latent_his(0)
            keep_latent(6)
            keep_latent(7)
            root_of(1)
            rope_swap(KEY)
            act.wait_ge(rope_rotated, 1)
            act.wait_ge(zeroed, 1)
            for h in range(2):
                half = slice(64 * h, 64 * h + 64)
                last = act.activation(kr_hi[half, h, :], rot[half, :], ACT.Copy)
            last.then_inc(rope_hi, 1)

            def proj_copy(pair, m, dst, b):
                act.wait_ge(proj_done, 6 * pair + m + 1)
                act.activation(dst, bank[:, b, :], ACT.Copy).then_inc(proj_hi, 1)

            def queries(pair):
                for h in range(2):
                    proj_copy(pair, h, q_hi[:, h, :], 6 + h)
                rope_swap(pair + 1)

            def rope_query_hi(pair):
                act.wait_ge(rope_rotated, pair + 2)
                act.activation(qr_hi[:, :], rot[:, :], ACT.Copy).then_inc(rope_hi, 1)

            def key(pair, h):
                proj_copy(pair, 2 + h, k_hi[:, h, :], 7 - h)

            def values(pair):
                for i in range(2):
                    proj_copy(pair, 4 + i, v_hi[:, 2 * i:2 * i + 2, :], 7 - i)

            def exps(pair, h):
                act.wait_ge(max_negated, 2 * pair + h + 1)
                for t in range(TT):
                    at, n = SCORE_AT[t], P * (t + 1)
                    last = act.activation(probs[:, h, at:at + n], score_bank(h)[:, at:at + n], ACT.Exp,
                                          bias=neg_max[:, h, t:t + 1], scale=SCALE, accum_out=row_sum[:, h, t:t + 1])
                last.then_inc(exped, 1)

            def prob_t_his(pair, h):
                act.wait_ge(transposed, 2 * pair + h + 1)
                for a, b in ((0, 512), (512, SCORE_COLS)):
                    act.activation(pt_hi[:, h, a:b], score_bank(h)[:, a:b], ACT.Copy).then_inc(pt_hi_made, 1)

            def head_out_hi(pair, h):
                act.wait_ge(pv_done, 2 * pair + h + 1)
                act.activation(act_hi[:, bass.ds(2 * pair + h, 1), :].rearrange("p o s -> p (o s)"), bank[:, 3 * h, :],
                               ACT.Copy).then_inc(o_hi_made, 1)

            def attention(pair, ahead):
                exps(pair, 0)
                exps(pair, 1)
                if ahead:
                    queries(pair + 1)
                prob_t_his(pair, 0)
                if ahead:
                    key(pair + 1, 0)
                    rope_query_hi(pair + 1)
                prob_t_his(pair, 1)
                if ahead:
                    key(pair + 1, 1)
                head_out_hi(pair, 0)
                head_out_hi(pair, 1)
                if ahead:
                    values(pair + 1)

            queries(0)
            rope_query_hi(0)
            latent_his(1)
            key(0, 0)
            key(0, 1)
            values(0)
            with act.Fori(0, PAIRS - 1) as pair:
                attention(pair, True)
            attention(PAIRS - 1, False)

            act.wait_ge(o_split, HEADS)
            for t in range(TT):
                act.dma_start(rows[:, t, :], x[t]).then_inc(rows_loaded[t], 16)
            for i in range(4):
                act.dma_start(ln_rows[:, i, :], ln[i].partition_broadcast(P)).then_inc(ln_loaded[i], 16)

            root_of(2)

            for k in range(KD):
                act.wait_ge(t_done, k + 1)
                if k >= 2:
                    act.wait_ge(t_split, k - 1)
                act.activation(two[:, k % 2, :], bank[:, 4 + k % 2, :], ACT.Identity,
                               scale=gains[:, 8 + k:9 + k], bias=gains[:, 8 + KD + k:9 + KD + k]).then_inc(t_affine, 1)

            def hidden(c, j):
                act.wait_ge(up_done, CHUNK * c + j + 1)
                b = j % 2
                if isinstance(c, int) and c == 0 and j < 2:
                    act.wait_ge(t_split, KD)
                else:
                    act.wait_ge(hid_squared, CHUNK * c + j - 1)
                act.activation(two[:, b, :], bank[:, 6 + b, :], ACT.Relu).then_inc(relu_made, 1)
                act.wait_ge(relu_made, CHUNK * c + j + 1)
                act.activation(mid_hi[:, j, :], two[:, b, :], ACT.Square).then_inc(hid_hi, 1)

            for j in range(CHUNK):
                hidden(0, j)
            with act.Fori(1, CHUNKS) as c:
                for j in range(CHUNK):
                    hidden(c, j)
            root_of(3)
            for t in range(TT):
                act.wait_ge(row_scaled, 2)
                act.activation(rows[:, t, :], rows[:, t, :], ACT.Identity, scale=rstd[:, t:t + 1],
                               bias=nmr[:, t:t + 1]).then_inc(out_gained, 1)

        @block.vector
        def _(dve):
            links = [0]

            def link(instruction):
                instruction.then_inc(dve_chain, 1)
                links[0] += 1
                dve.wait_ge(dve_chain, links[0])

            def inv_root(n, src, scale, eps):
                dve.tensor_scalar(ssq, src, scale, eps, ALU.mult, ALU.add).then_inc(var_made, 1)
                dve.wait_ge(root_made, n + 1)
                link(dve.reciprocal(inv, root))
                link(dve.tensor_tensor(tmp, inv, inv, ALU.mult))
                link(dve.tensor_tensor(tmp, tmp, ssq, ALU.mult))
                link(dve.tensor_scalar(tmp, tmp, -0.5, 1.5, ALU.mult, ALU.add))
                link(dve.tensor_tensor(rstd, inv, tmp, ALU.mult))

            dve.memset(ones[:, :], 1.0).then_inc(consts_made, 1)
            for k in range(KD):
                dve.wait_ge(x_hi_made, k + 1)
                dve.tensor_tensor(act_lo[:, k, :], x_raw[:, k, :], act_hi[:, k, :].bitcast(f32), ALU.subtract)\
                   .then_inc(x_split, 1)
            dve.wait_ge(x_split, KD)
            for part in (kr_hi, kr_lo):
                for h in range(2):
                    last = dve.memset(part[64 - 64 * h:128 - 64 * h, h, :].bitcast(f32), 0.0)
            last.then_inc(zeroed, 1)

            def scale_latent(g):
                dve.wait_ge(ssq_done, g + 1)
                if g:
                    dve.wait_ge(inv_spread, g)
                inv_root(g, bank[:, 2, TT * g:TT * g + TT], 1.0 / LORA, RMS_EPS)
                for t in range(TT):
                    last = dve.tensor_scalar(diag[:, t, :], ident, rstd[:, t:t + 1], None, ALU.mult)
                last.then_inc(diag_made, 1)
                dve.wait_ge(inv_spread, g + 1)
                for j in range(KL * g, KL * g + KL):
                    dve.scalar_tensor_tensor(out=latent[:, j, :], in0=latent[:, j, :], scalar=gains[:, j:j + 1],
                                             in1=bank[:, 3, :], op0=ALU.mult, op1=ALU.mult).then_inc(latent_scaled, 1)

            def latent_los(g):
                for j in range(KL * g, KL * g + KL):
                    dve.wait_ge(latent_hi, j + 1)
                    dve.tensor_tensor(mid_lo[:, j, :], latent[:, j, :], mid_hi[:, j, :].bitcast(f32), ALU.subtract)\
                       .then_inc(latent_split, 1)

            KEY = 0

            def rotate(r, b):
                dve.wait_ge(rope_swapped, r + 1)
                if r is not KEY:
                    dve.wait_ge(rope_split, r)
                dve.tensor_tensor(rot[:, :], bank[:, b, :], rope_cos, ALU.mult).then_inc(rope_cosined, 1)
                dve.tensor_tensor(swap[:, :], swap[:, :], rope_sin, ALU.mult).then_inc(rope_sined, 1)
                dve.wait_ge(rope_cosined, r + 1)
                dve.wait_ge(rope_sined, r + 1)
                dve.tensor_tensor(rot[:, :], rot[:, :], swap[:, :], ALU.add).then_inc(rope_rotated, 1)

            dve.wait_ge(gains_loaded, 16)
            scale_latent(0)
            latent_los(0)
            scale_latent(1)
            rotate(KEY, 0)
            dve.wait_ge(rope_hi, 1)
            for h in range(2):
                half = slice(64 * h, 64 * h + 64)
                last = dve.tensor_tensor(kr_lo[half, h, :], rot[half, :], kr_hi[half, h, :].bitcast(f32), ALU.subtract)
            last.then_inc(rope_split, 1)

            def proj_rest(pair, m, lo, hi, b):
                dve.wait_ge(proj_hi, 6 * pair + m + 1)
                dve.tensor_tensor(lo, bank[:, b, :], hi.bitcast(f32), ALU.subtract).then_inc(proj_split, 1)

            def queries(pair):
                for h in range(2):
                    proj_rest(pair, h, q_lo[:, h, :], q_hi[:, h, :], 6 + h)
                rotate(pair + 1, 6)

            def rope_query_lo(pair):
                dve.wait_ge(rope_hi, pair + 2)
                dve.tensor_tensor(qr_lo[:, :], rot[:, :], qr_hi[:, :].bitcast(f32), ALU.subtract).then_inc(rope_split, 1)

            def key(pair, h):
                proj_rest(pair, 2 + h, k_lo[:, h, :], k_hi[:, h, :], 7 - h)

            def values(pair):
                for i in range(2):
                    part = slice(2 * i, 2 * i + 2)
                    proj_rest(pair, 4 + i, v_lo[:, part, :].rearrange("p t d -> p (t d)"),
                              v_hi[:, part, :].rearrange("p t d -> p (t d)"), 7 - i)

            def maxima(pair, h):
                dve.wait_ge(scored, 2 * pair + h + 1)
                for t in range(TT):
                    at, n = SCORE_AT[t], P * (t + 1)
                    last = dve.reduce_max(row_max[:, h, t:t + 1], score_bank(h)[:, at:at + n], AX.X)
                last.then_inc(maxed, 1)
                dve.wait_ge(maxed, 2 * pair + h + 1)
                dve.tensor_scalar(neg_max[:, h, :], row_max[:, h, :], -SCALE, None, ALU.mult).then_inc(max_negated, 1)

            def normalise(pair, h):
                dve.wait_ge(exped, 2 * pair + h + 1)
                dve.reciprocal(inv_sum[:, h, :], row_sum[:, h, :]).then_inc(sum_inverted, 1)
                dve.wait_ge(sum_inverted, 2 * pair + h + 1)
                for t in range(TT):
                    at, n = SCORE_AT[t], P * (t + 1)
                    last = dve.tensor_scalar(probs[:, h, at:at + n], probs[:, h, at:at + n], inv_sum[:, h, t:t + 1],
                                             None, ALU.mult)
                last.then_inc(normed, 1)

            def prob_t_los(pair, h):
                for i, (a, b) in enumerate(((0, 512), (512, SCORE_COLS))):
                    dve.wait_ge(pt_hi_made, 4 * pair + 2 * h + i + 1)
                    dve.tensor_tensor(pt_lo[:, h, a:b], score_bank(h)[:, a:b], pt_hi[:, h, a:b].bitcast(f32),
                                      ALU.subtract).then_inc(pt_split, 1)

            def head_out_lo(pair, h):
                dve.wait_ge(o_hi_made, 2 * pair + h + 1)
                head = bass.ds(2 * pair + h, 1)
                dve.tensor_tensor(act_lo[:, head, :].rearrange("p o s -> p (o s)"), bank[:, 3 * h, :],
                                  act_hi[:, head, :].rearrange("p o s -> p (o s)").bitcast(f32), ALU.subtract)\
                   .then_inc(o_split, 1)

            def attention(pair, ahead):
                maxima(pair, 0)
                maxima(pair, 1)
                normalise(pair, 0)
                normalise(pair, 1)
                if ahead:
                    queries(pair + 1)
                prob_t_los(pair, 0)
                if ahead:
                    key(pair + 1, 0)
                    rope_query_lo(pair + 1)
                prob_t_los(pair, 1)
                if ahead:
                    key(pair + 1, 1)
                head_out_lo(pair, 0)
                head_out_lo(pair, 1)
                if ahead:
                    values(pair + 1)

            queries(0)
            rope_query_lo(0)
            latent_los(1)
            key(0, 0)
            key(0, 1)
            values(0)
            with dve.Fori(0, PAIRS - 1) as pair:
                attention(pair, True)
            attention(PAIRS - 1, False)

            def row_bank(cg, t):
                return bank[:, t + (4 if cg % 2 == 0 else 0), :]

            def add_rows(rnd, cg):
                for t in range(TT):
                    dve.wait_ge(block_done, 16 * rnd + 4 * cg + t + 1)
                    part = rows[:, t, 512 * cg:512 * cg + 512]
                    scale = ALPHA if isinstance(rnd, int) and rnd == 0 else 1.0
                    dve.scalar_tensor_tensor(out=part, in0=part, scalar=scale, in1=row_bank(cg, t), op0=ALU.mult,
                                             op1=ALU.add).then_inc(rows_added, 1)

            def measure(rnd, cg):
                for t in range(TT):
                    dve.wait_ge(rows_added, 16 * rnd + 4 * cg + t + 1)
                    last = dve.bn_stats(stats[:, t, cg, :], rows[:, t, 512 * cg:512 * cg + 512])
                last.then_inc(row_stats, 1)

            def aggregate(n):
                dve.wait_ge(row_stats, 4 * n + 4)
                for t in range(TT):
                    last = dve.bn_aggr(moments[:, t, :], stats[:, t, :, :].rearrange("p c s -> p (c s)"))
                link(last)
                inv_root(2 + n, moments[:, :, 1], 1.0, LN_EPS)
                link(dve.tensor_tensor(tmp, moments[:, :, 0], rstd, ALU.mult))
                dve.tensor_scalar(nmr, tmp, -1.0, None, ALU.mult).then_inc(row_scaled, 1)

            for t in range(TT):
                dve.wait_ge(rows_loaded[t], 16)
            for cg in range(CG):
                add_rows(0, cg)
                measure(0, cg)
            aggregate(0)
            dve.wait_ge(row_scaled, 1)
            for cg in range(CG):
                for t in range(TT):
                    part = rows[:, t, 512 * cg:512 * cg + 512]
                    last = dve.tensor_scalar(part, part, rstd[:, t:t + 1], nmr[:, t:t + 1], ALU.mult, ALU.add)
                last.then_inc(normed, 1)
            for k in range(KD):
                dve.wait_ge(t_affine, k + 1)
                dve.tensor_copy(act_hi[:, k, :], two[:, k % 2, :]).then_inc(t_hi, 1)
                dve.wait_ge(t_hi, k + 1)
                dve.tensor_tensor(act_lo[:, k, :], two[:, k % 2, :], act_hi[:, k, :].bitcast(f32), ALU.subtract)\
                   .then_inc(t_split, 1)

            def hidden(c, j):
                b = bank[:, 6 + j % 2, :]
                dve.wait_ge(relu_made, CHUNK * c + j + 1)
                dve.scalar_tensor_tensor(out=b, in0=b, scalar=0.0, in1=two[:, j % 2, :], op0=ALU.max, op1=ALU.mult)\
                   .then_inc(hid_squared, 1)
                dve.wait_ge(hid_squared, CHUNK * c + j + 1)
                dve.wait_ge(hid_hi, CHUNK * c + j + 1)
                dve.tensor_tensor(mid_lo[:, j, :], b, mid_hi[:, j, :].bitcast(f32), ALU.subtract).then_inc(hid_split, 1)

            def residual(i):
                t, half = i // 2, slice(1024 * (i % 2), 1024 * (i % 2) + 1024)
                part = rows[:, t, half]
                dve.scalar_tensor_tensor(out=part, in0=part, scalar=ALPHA, in1=ln_rows[:, 0, half], op0=ALU.mult,
                                         op1=ALU.mult).then_inc(residual_scaled, 1)
                dve.wait_ge(residual_scaled, i + 1)
                dve.scalar_tensor_tensor(out=part, in0=ln_rows[:, 1, half], scalar=ALPHA, in1=part, op0=ALU.mult,
                                         op1=ALU.add).then_inc(residual_made, 1)

            dve.wait_ge(ln_loaded[0], 16)
            dve.wait_ge(ln_loaded[1], 16)
            dve.wait_ge(t_done, KD)
            for j in range(CHUNK):
                hidden(0, j)
                residual(j)
            dve.wait_ge(residual_made, 8)
            for cg in range(CG):
                add_rows(1, cg)
            with dve.Fori(1, CHUNKS - 1) as c:
                for j in range(CHUNK):
                    hidden(c, j)
                for cg in range(CG):
                    add_rows(c + 1, cg)
            for j in range(CHUNK):
                hidden(CHUNKS - 1, j)
            for cg in range(CG):
                add_rows(CHUNKS, cg)
                measure(CHUNKS, cg)
            aggregate(1)
            dve.wait_ge(ln_loaded[2], 16)
            dve.wait_ge(ln_loaded[3], 16)
            for t in range(TT):
                dve.wait_ge(out_gained, t + 1)
                link(dve.tensor_tensor(rows[:, t, :], rows[:, t, :], ln_rows[:, 2, :], ALU.mult))
                dve.tensor_tensor(rows[:, t, :], rows[:, t, :], ln_rows[:, 3, :], ALU.add).then_inc(out_made, 1)

        @block.tensor
        def _(pe):
            read_out = [0]

            def weights_read():
                read_out[0] += 1

            def product(out_, a_hi, a_lo, b_hi, b_lo, start, stop):
                first_pass = pe.matmul(out_, a_hi, b_hi, start=start, stop=False)
                if read_out[0]:
                    first_pass.then_inc(w_used, read_out[0])
                    read_out[0] = 0
                pe.matmul(out_, a_hi, b_lo, start=False, stop=False)
                return pe.matmul(out_, a_lo, b_hi, start=False, stop=stop)

            def stream_tile(n, slot, dst, ready=None):
                for half in range(2):
                    s = (slot + half) % SLOTS
                    pe.wait_ge(w_split, n + half + 1)
                    for kk in range(KD // 2):
                        k = half * KD // 2 + kk
                        if ready:
                            ready(k)
                        cols = slice(P * kk, P * kk + P)
                        last = product(dst, w_hi[:, s, cols], w_lo[:, s, cols], act_hi[:, k, :], act_lo[:, k, :],
                                       k == 0, k == KD - 1)
                    weights_read()
                return last

            def in_tile(j, b):
                if not (isinstance(j, int) and j < 2):
                    pe.wait_ge(latent_kept, j - 1)
                last = stream_tile(2 * j, 2 * b, bank[:, b, :])
                return last

            def sum_squares(g):
                pe.wait_ge(latent_kept, KL * g + KL)
                for t in range(TT):
                    for j in range(KL):
                        last = pe.matmul(bank[:, 2, TT * g + t:TT * g + t + 1], square[:, j, P * t:P * t + P], ones[:, 0:1],
                                         start=j == 0, stop=j == KL - 1)
                last.then_inc(ssq_done, 1)

            def spread_inverse(g):
                pe.wait_ge(diag_made, g + 1)
                if g:
                    pe.wait_ge(latent_scaled, KL)
                for t in range(TT):
                    last = pe.matmul(bank[:, 3, P * t:P * t + P], ones[:, :], diag[:, t, :], start=True, stop=True)
                last.then_inc(inv_spread, 1)

            for j in range(2):
                def x_ready(k, j=j):
                    if j == 0:
                        pe.wait_ge(x_split, k + 1)
                last = stream_tile(2 * j, 2 * j, bank[:, j, :], x_ready)
                last.then_inc(in_done, 1)
            with pe.Fori(1, 3) as i:
                for b in range(2):
                    in_tile(2 * i + b, b).then_inc(in_done, 1)
            pe.wait_ge(consts_made, 2)
            sum_squares(0)
            in_tile(6, 0).then_inc(in_done, 1)
            spread_inverse(0)
            in_tile(7, 1).then_inc(in_done, 1)
            pe.wait_ge(latent_kept, 7)

            def squares_midway(k):
                if k == 10:
                    sum_squares(1)
            stream_tile(16, 0, bank[:, 0, :], squares_midway).then_inc(rope_done, 1)

            def head_tile(pair, hb, at, lat, dst, width=P):
                s = (HB_QKV + hb) % SLOTS
                pe.wait_ge(w_split, HB_QKV + QKV_HB * pair + hb + 1)
                for k in range(KL):
                    cols = slice(at + width * k, at + width * k + P)
                    last = product(dst, w_hi[:, s, cols], w_lo[:, s, cols], mid_hi[:, lat + k, :], mid_lo[:, lat + k, :],
                                   k == 0, k == KL - 1)
                return last

            def first(pair):
                return isinstance(pair, int) and pair == 0

            def query(pair, h):
                if first(pair):
                    pe.wait_ge(latent_split, KL)
                else:
                    pe.wait_ge(proj_split, 6 * pair - h)
                last = head_tile(pair, 0, KL * P * h, 0, bank[:, 6 + h, :])
                last.then_inc(proj_done, 1)
                if h:
                    weights_read()

            def rope_query(pair):
                pe.wait_ge(proj_split, 6 * pair + 1)
                head_tile(pair, 1, 0, 0, bank[:, 6, :]).then_inc(rope_done, 1)
                weights_read()

            def key(pair, h):
                if h == 0:
                    if first(pair):
                        pe.wait_ge(latent_split, 2 * KL)
                    pe.wait_ge(proj_split, 6 * pair + 2)
                else:
                    pe.wait_ge(rope_rotated, pair + 2)
                head_tile(pair, 2, KL * P * h, KL, bank[:, 7 - h, :]).then_inc(proj_done, 1)
                if h:
                    weights_read()

            def value(pair, i):
                s = (HB_QKV + 3) % SLOTS
                pe.wait_ge(w_split, HB_QKV + QKV_HB * pair + 4)
                pe.wait_ge(proj_split, 6 * pair + 3 + i)
                for half in range(2):
                    tok = slice(P * (2 * i + half), P * (2 * i + half) + P)
                    for k in range(KL):
                        cols = slice(2 * VDIM * k, 2 * VDIM * k + 2 * VDIM)
                        last = product(bank[:, 7 - i, 256 * half:256 * half + 256], mid_hi[:, KL + k, tok],
                                       mid_lo[:, KL + k, tok], w_hi[:, s, cols], w_lo[:, s, cols], k == 0, k == KL - 1)
                last.then_inc(proj_done, 1)
                if i:
                    weights_read()

            def scores(pair, h):
                if h == 0:
                    pe.wait_ge(proj_split, 6 * pair + 4)
                    pe.wait_ge(rope_split, pair + 2)
                if not first(pair):
                    pe.wait_ge(o_split, 2 * pair + h - 1)
                for t in range(TT):
                    q, keys = slice(P * t, P * t + P), slice(0, P * (t + 1))
                    dst = score_bank(h)[:, SCORE_AT[t]:SCORE_AT[t] + P * (t + 1)]
                    product(dst, q_hi[:, h, q], q_lo[:, h, q], k_hi[:, h, keys], k_lo[:, h, keys], True, False)
                    product(dst, qr_hi[:, q], qr_lo[:, q], kr_hi[:, h, keys], kr_lo[:, h, keys], False, False)
                    last = pe.matmul(dst[:, P * t:P * t + P], ident_r[:, :], mask_r[:, :], start=False, stop=True)
                last.then_inc(scored, 1)

            def transpose_probs(pair, h):
                pe.wait_ge(normed, 2 * pair + h + 1)
                for k in range(TT):
                    for t in range(k, TT):
                        at = PROB_T_AT[k] + P * (t - k)
                        last = pe.transpose(score_bank(h)[:, at:at + P],
                                            probs[:, h, SCORE_AT[t] + P * k:SCORE_AT[t] + P * k + P], ident)
                last.then_inc(transposed, 1)

            def weigh_values(pair, h):
                if h == 0:
                    pe.wait_ge(proj_split, 6 * pair + 6)
                pe.wait_ge(pt_split, 4 * pair + 2 * h + 2)
                for k in range(TT):
                    at, n = PROB_T_AT[k], S - P * k
                    v = slice(VDIM * h, VDIM * h + VDIM)
                    last = product(bank[:, 3 * h, P * k:S], v_hi[:, k, v], v_lo[:, k, v], pt_hi[:, h, at:at + n],
                                   pt_lo[:, h, at:at + n], k == 0, k == TT - 1)
                last.then_inc(pv_done, 1)

            def attention(pair, ahead):
                scores(pair, 0)
                scores(pair, 1)
                if ahead:
                    query(pair + 1, 0)
                    query(pair + 1, 1)
                    rope_query(pair + 1)
                transpose_probs(pair, 0)
                if ahead:
                    key(pair + 1, 0)
                transpose_probs(pair, 1)
                if ahead:
                    key(pair + 1, 1)
                    value(pair + 1, 0)
                weigh_values(pair, 0)
                weigh_values(pair, 1)
                if ahead:
                    value(pair + 1, 1)

            query(0, 0)
            query(0, 1)
            spread_inverse(1)
            rope_query(0)
            key(0, 0)
            key(0, 1)
            value(0, 0)
            value(0, 1)
            attention(0, True)
            with pe.Fori(1, PAIRS - 1) as pair:
                attention(pair, True)
            attention(PAIRS - 1, False)

            def row_block(rnd, cg, parity, m, n, src_hi, src_lo, last_m):
                s = (HB_O + m) % SLOTS
                pe.wait_ge(w_split, n + 1)
                for t in range(TT):
                    dst = bank[:, t + (0 if parity else 4), :]
                    if m == 0 and not (isinstance(rnd, int) and rnd == 0 and cg < 2):
                        if parity == 0 and isinstance(cg, int) and cg == 0:
                            if t >= 2:
                                pe.wait_ge(hid_split, CHUNK * (rnd - 1) + 5 + t)
                        else:
                            pe.wait_ge(rows_added, 16 * rnd + 4 * cg - 8 + t + 1)
                    for kk in range(2):
                        k = 2 * m + kk
                        tok = slice(P * t, P * t + P)
                        cols = slice(512 * kk, 512 * kk + 512)
                        last = product(dst, src_hi[:, k, tok], src_lo[:, k, tok], w_hi[:, s, cols], w_lo[:, s, cols],
                                       k == 0, m == last_m and kk == 1)
                    if m == last_m:
                        last.then_inc(block_done, 1)
                weights_read()

            for cg in range(CG):
                for m in range(KD // 2):
                    if cg == 0 and m == KD // 2 - 1:
                        pe.wait_ge(o_split, HEADS)
                    row_block(0, cg, cg % 2, m, HB_O + KD // 2 * cg + m, act_hi, act_lo, KD // 2 - 1)

            def transpose_rows(k):
                if k % 4 == 0:
                    pe.wait_ge(normed, HEADS + k // 4 + 1)
                if k >= 2:
                    pe.wait_ge(t_split, k - 1)
                for t in range(TT):
                    last = pe.transpose(bank[:, 4 + k % 2, P * t:P * t + P], rows[:, t, P * k:P * k + P], ident)
                last.then_inc(t_done, 1)

            def up_tile(c, j, b, ready=None):
                if isinstance(j, int) and j < 2:
                    pe.wait_ge(rows_added, 16 * c + 12)
                else:
                    pe.wait_ge(hid_split, CHUNK * c + j - 1)
                n = HB_MLP + MLP_HB * c + 2 * j
                stream_tile(n, (HB_MLP + 2 * b) % SLOTS, bank[:, 6 + b, :], ready).then_inc(up_done, 1)

            def down(c):
                n = HB_MLP + MLP_HB * c + UP_HB
                for cg in range(CG):
                    for m in range(CHUNK // 2):
                        if cg == 0:
                            pe.wait_ge(hid_split, CHUNK * c + 2 * m + 2)
                        row_block(c + 1, cg, cg % 2, m, n + CHUNK // 2 * cg + m, mid_hi, mid_lo, CHUNK // 2 - 1)

            def first_ready(k):
                if k == 0:
                    transpose_rows(0)
                    transpose_rows(1)
                if k + 2 < KD:
                    transpose_rows(k + 2)
                pe.wait_ge(t_split, k + 1)

            up_tile(0, 0, 0, first_ready)
            up_tile(0, 1, 1)
            with pe.Fori(1, CHUNK // 2) as i:
                for b in range(2):
                    up_tile(0, 2 * i + b, b)
            down(0)
            with pe.Fori(1, CHUNKS) as c:
                for b in range(2):
                    up_tile(c, b, b)
                with pe.Fori(1, CHUNK // 2) as i:
                    for b in range(2):
                        up_tile(c, 2 * i + b, b)
                down(c)


def _stream(w_in, w_uq, w_ukv, w_o, w1, w2):
    import numpy as np
    out = np.zeros((N_HB, P, HB), np.float32)
    w_in = np.concatenate([w_in[:, :2 * LORA], w_in[:, 2 * LORA:], w_in[:, 2 * LORA:]], axis=1)
    out[:IN_HB] = w_in.reshape(2, KD // 2, P, IN_TILES, P).transpose(3, 0, 2, 1, 4).reshape(IN_HB, P, HB)
    qkv = out[HB_QKV:HB_O].reshape(PAIRS, QKV_HB, P, HB)
    uq = w_uq.reshape(KL, P, PAIRS, 2, NOPE + ROPE)
    qkv[:, 0] = uq[..., :NOPE].transpose(2, 1, 3, 0, 4).reshape(PAIRS, P, HB)
    qkv[:, 1, :, :HB // 2] = uq[..., NOPE:].transpose(2, 1, 0, 3, 4).reshape(PAIRS, P, HB // 2)
    ukv = w_ukv.reshape(KL, P, PAIRS, 2, NOPE + VDIM)
    qkv[:, 2] = ukv[..., :NOPE].transpose(2, 1, 3, 0, 4).reshape(PAIRS, P, HB)
    qkv[:, 3] = ukv[..., NOPE:].transpose(2, 1, 0, 3, 4).reshape(PAIRS, P, HB)
    out[HB_O:HB_MLP] = w_o.reshape(KD // 2, 2, P, CG, 512).transpose(3, 0, 2, 1, 4).reshape(O_HB, P, HB)
    mlp = out[HB_MLP:].reshape(CHUNKS, MLP_HB, P, HB)
    mlp[:, :UP_HB] = w1.reshape(2, KD // 2, P, CHUNKS, CHUNK, P).transpose(3, 4, 0, 2, 1, 5)\
        .reshape(CHUNKS, UP_HB, P, HB)
    mlp[:, UP_HB:] = w2.reshape(CHUNKS, CHUNK // 2, 2, P, CG, 512).transpose(0, 4, 1, 3, 2, 5)\
        .reshape(CHUNKS, DOWN_HB, P, HB)
    return out


def _tables():
    import numpy as np
    inv = (1.0 / (np.float32(10000.0) ** (np.arange(0, ROPE, 2, dtype=np.float32) / np.float32(ROPE)))).astype(np.float32)
    ang = inv[:, None] * np.arange(S, dtype=np.float32)[None, :]
    cos, sin = np.cos(ang).astype(np.float32), np.sin(ang).astype(np.float32)
    ident = np.eye(P, dtype=np.float32)
    mask = np.where(np.arange(P)[None, :] <= np.arange(P)[:, None], 0.0, MASKED).astype(np.float32)
    return np.ascontiguousarray(np.concatenate(
        [ident, mask, np.concatenate([cos] * 4), np.concatenate([-sin, sin] * 2)], axis=1))


def kernel(x, mla_w_in, mla_q_norm, mla_kv_norm, mla_w_uq, mla_w_ukv, mla_w_o,
           hgrn_w_in, hgrn_lb_logits, hgrn_o_norm, hgrn_w_o, sb_w_in, sb_w_o, moba_w_in, moba_w_o,
           ln_g, ln_b, mlp_w1, mlp_w2):
    import numpy as np
    import concourse.bacc as _bacc
    from concourse.bass_utils import run_bass_kernel_spmd as _run

    x = np.asarray(x)[0]
    arrays = {
        "x_t": np.ascontiguousarray(x.T.reshape(KD, P, S).transpose(1, 0, 2)),
        "x_rows": np.ascontiguousarray(x.reshape(TT, P, D)),
        "weights": _stream(*(np.asarray(a)[0] for a in (mla_w_in, mla_w_uq, mla_w_ukv, mla_w_o, mlp_w1, mlp_w2))),
        "tables": _tables(),
        "gains": np.ascontiguousarray(np.concatenate(
            [np.asarray(a).reshape(-1, P).T for a in (mla_q_norm[0], mla_kv_norm[0], ln_g[0, 0], ln_b[0, 0])], axis=1)),
        "ln": np.ascontiguousarray(np.stack([np.asarray(a) for a in (ln_g[0, 0], ln_b[0, 0], ln_g[0, 1], ln_b[0, 1])])),
    }
    nc = _bacc.Bacc("TRN2", target_bir_lowering=False, num_devices=1)
    args = [nc.dram_tensor(name, a.shape, mybir.dt.float32, kind="ExternalInput").ap() for name, a in arrays.items()]
    out = nc.dram_tensor("out_rows", (TT, P, D), mybir.dt.float32, kind="ExternalOutput").ap()
    mla_mlp_program(nc, *args, out)
    r = _run(nc, [arrays], core_ids=[0])
    return r.results[0]["out_rows"].reshape(1, S, D)
```

```python
import concourse.bass as bass
from concourse import mybir
from contextlib import ExitStack

P = 128
D = 2048
S = 512
KD = D // P
TT = S // P
LORA = 512
KL = LORA // P
HEADS = 16
PAIRS = HEADS // 2
NOPE, ROPE, VDIM = 128, 64, 128
FF = 4 * D
CHUNK = 8
CHUNKS = FF // P // CHUNK
CG = D // 512
ALPHA = 2.0 ** 0.25
SCALE = (NOPE + ROPE) ** -0.5
LN_EPS, RMS_EPS = 1e-5, 1e-6
MASKED = -1e30

HB = 1024
IN_TILES = 2 * KL + 1
IN_HB = 2 * IN_TILES
QKV_HB = 4
HB_QKV = IN_HB
HB_O = HB_QKV + QKV_HB * PAIRS
O_HB = CG * KD // 2
HB_MLP = HB_O + O_HB
UP_HB = 2 * CHUNK
DOWN_HB = CG * CHUNK // 2
MLP_HB = UP_HB + DOWN_HB
N_HB = HB_MLP + CHUNKS * MLP_HB
SLOTS = 4
RAWS = 2

SCORE_AT = {0: 0, 2: 128, 3: 512, 1: 1024}
PROB_T_AT = {0: 0, 1: 512, 3: 896, 2: 1024}
SCORE_COLS = 1280


def mla_mlp_program(nc, xT, x, w, const, gain, ln, out):
    f32, f32r = mybir.dt.float32, mybir.dt.float32r
    ALU, ACT, AX = mybir.AluOpType, mybir.ActivationFunctionType, mybir.AxisListType

    with ExitStack() as ctx:
        arena = ctx.enter_context(nc.sbuf_tensor("arena", [P, 53200], f32))
        base = nc.sbuf_base - 53200 * 4
        place = [base]

        def sb(name, shape, dt=f32, at=None):
            size = 4
            for n in shape[1:]:
                size *= n
            if at is None:
                at = place[0]
                place[0] += size
            assert at + size <= base + 53200 * 4, name
            return nc.alloc_sbuf_tensor_at(name, shape, dt, offset=at)

        def sem(name):
            return ctx.enter_context(nc.semaphore(name))

        act_hi, act_lo = sb("act_hi", [P, KD, S], f32r), sb("act_lo", [P, KD, S], f32r)
        mid_hi, mid_lo = sb("mid_hi", [P, 8, S], f32r), sb("mid_lo", [P, 8, S], f32r)
        raw = sb("raw", [P, RAWS, HB])
        w_hi, w_lo = sb("w_hi", [P, SLOTS, HB], f32r), sb("w_lo", [P, SLOTS, HB], f32r)
        table = sb("table", [P, 2 * P + 2 * S])
        ident = table[:, 0:P]
        mask = table[:, P:2 * P]
        rope_cos = table[:, 2 * P:2 * P + S]
        rope_sin = table[:, 2 * P + S:2 * P + 2 * S]
        two = table[:, 2 * P:2 * P + 2 * S].rearrange("p (a s) -> p a s", a=2)
        ident_r, mask_r = sb("ident_r", [P, P], f32r), sb("mask_r", [P, P], f32r)
        ones = sb("ones", [P, P])
        gains = sb("gains", [P, 8 + 2 * KD])
        small = sb("small", [P, 160])
        ssq, root, inv, tmp, rstd = (small[:, 4 * i:4 * i + 4] for i in range(5))
        all_roots = (ssq, root, inv, tmp, rstd)
        nmr = small[:, 20:24]
        moments = small[:, 24:32].rearrange("p (t m) -> p t m", m=2)
        row_max = small[:, 32:40].rearrange("p (h t) -> p h t", h=2)
        neg_max = small[:, 40:48].rearrange("p (h t) -> p h t", h=2)
        row_sum = small[:, 48:56].rearrange("p (h t) -> p h t", h=2)
        inv_sum = small[:, 56:64].rearrange("p (h t) -> p h t", h=2)
        stats = small[:, 64:160].rearrange("p (t c s) -> p t c s", t=TT, c=CG)
        overlay = place[0]

        probs = sb("probs", [P, 2, SCORE_COLS])
        pt_hi = sb("pt_hi", [P, 2, SCORE_COLS], f32r)
        pt_lo = sb("pt_lo", [P, 2, SCORE_COLS], f32r)
        load_area = place[0]
        k_hi, k_lo = sb("k_hi", [P, 2, S], f32r), sb("k_lo", [P, 2, S], f32r)
        qr_hi, qr_lo = sb("qr_hi", [P, S], f32r), sb("qr_lo", [P, S], f32r)
        kr_hi, kr_lo = sb("kr_hi", [P, 2, S], f32r), sb("kr_lo", [P, 2, S], f32r)
        v_hi, v_lo = sb("v_hi", [P, TT, 2 * VDIM], f32r), sb("v_lo", [P, TT, 2 * VDIM], f32r)
        rot, swap = sb("rot", [P, S]), sb("swap", [P, S])
        q_hi, q_lo = act_hi[:, HEADS - 2:HEADS, :], act_lo[:, HEADS - 2:HEADS, :]
        x_raw = sb("x_raw", [P, KD, S], at=load_area)
        latent = sb("latent", [P, 2 * KL, S], at=overlay)
        square = sb("square", [P, KL, S], at=overlay + 4 * 2 * KL * S)
        diag = sb("diag", [P, TT, P], at=overlay + 4 * 3 * KL * S)
        rows = sb("rows", [P, TT, D], at=overlay)
        ln_rows = sb("ln_rows", [P, 4, D], at=overlay + 4 * TT * D)

        bank = ctx.enter_context(nc.psum_tensor("bank", [P, 8, 512], f32))

        def score_bank(h):
            return bank[:, 3 * h:3 * h + 3, :].rearrange("p b n -> p (b n)")

        x_loaded = [sem(f"x_loaded{i}") for i in range(KD // 2)]
        table_loaded, gains_loaded = sem("table_loaded"), sem("gains_loaded")
        rows_loaded = [sem(f"rows_loaded{t}") for t in range(TT)]
        ln_loaded = [sem(f"ln_loaded{i}") for i in range(4)]
        stored = [sem(f"stored{t}") for t in range(TT)]
        raw_loaded = [sem(f"raw_loaded{i}") for i in range(RAWS)]
        w_hi_made, w_split, w_used = sem("w_hi_made"), sem("w_split"), sem("w_used")
        x_hi_made, x_split = sem("x_hi_made"), sem("x_split")
        consts_made = sem("consts_made")
        in_done, latent_kept, squared = sem("in_done"), sem("latent_kept"), sem("squared")
        ssq_done, var_made, root_made, dve_chain = sem("ssq_done"), sem("var_made"), sem("root_made"), sem("dve_chain")
        diag_made, inv_spread = sem("diag_made"), sem("inv_spread")
        latent_scaled, latent_hi, latent_split = sem("latent_scaled"), sem("latent_hi"), sem("latent_split")
        rope_done, rope_swapped, rope_cosined = sem("rope_done"), sem("rope_swapped"), sem("rope_cosined")
        rope_sined, rope_rotated, rope_hi, rope_split = sem("rope_sined"), sem("rope_rotated"), sem("rope_hi"), sem("rope_split")
        zeroed = sem("zeroed")
        proj_done, proj_hi, proj_split = sem("proj_done"), sem("proj_hi"), sem("proj_split")
        scored, maxed, max_negated = sem("scored"), sem("maxed"), sem("max_negated")
        exped, sum_inverted, normed = sem("exped"), sem("sum_inverted"), sem("normed")
        transposed, pt_hi_made, pt_split = sem("transposed"), sem("pt_hi_made"), sem("pt_split")
        pv_done, o_hi_made, o_split = sem("pv_done"), sem("o_hi_made"), sem("o_split")
        block_done, rows_added, row_stats = sem("block_done"), sem("rows_added"), sem("row_stats")
        row_scaled, t_done, t_affine, t_hi, t_split = sem("row_scaled"), sem("t_done"), sem("t_affine"), sem("t_hi"), sem("t_split")
        residual_scaled, residual_made = sem("residual_scaled"), sem("residual_made")
        up_done, relu_made, hid_hi, hid_squared, hid_split = sem("up_done"), sem("relu_made"), sem("hid_hi"), sem("hid_squared"), sem("hid_split")
        row_normed, gained = sem("row_normed"), sem("gained")
        pool_gained = sem("pool_gained")
        out_made = [sem(f"out_made{t}") for t in range(TT)]

        block = ctx.enter_context(nc.Block())

        @block.sync
        def _(sp):
            def load_x(i):
                sp.dma_start(x_raw[:, 2 * i:2 * i + 2, :], xT[:, 2 * i:2 * i + 2, :]).then_inc(x_loaded[i], 16)

            sp.dma_start(raw[:, 0, :], w[0]).then_inc(raw_loaded[0], 16)
            load_x(0)
            load_x(1)
            sp.dma_start(raw[:, 1, :], w[1]).then_inc(raw_loaded[1], 16)
            for i in range(2, KD // 2):
                load_x(i)
            with sp.Fori(1, N_HB // RAWS) as i:
                for s in range(RAWS):
                    sp.wait_ge(w_split, RAWS * i + s - RAWS + 1)
                    sp.dma_start(raw[:, s, :], w[bass.ds(RAWS * i + s, 1)].rearrange("o p n -> (o p) n"))\
                      .then_inc(raw_loaded[s], 16)
            for t in range(TT):
                for half in range(2):
                    cols = slice(D // 2 * half, D // 2 * half + D // 2)
                    sp.wait_ge(out_made[t], half + 1)
                    sp.dma_start(out[t][:, cols], rows[:, t, cols]).then_inc(stored[t], 16)
            for t in range(TT):
                sp.wait_ge(stored[t], 32)

        @block.gpsimd
        def _(pool):
            def rest(turn, s):
                pool.wait_ge(w_hi_made, SLOTS * turn + s + 1)
                pool.tensor_tensor(w_lo[:, s, :], raw[:, s % RAWS, :], w_hi[:, s, :].bitcast(f32), ALU.subtract)\
                    .then_inc(w_split, 1)

            with pool.Fori(0, N_HB // SLOTS) as turn:
                for s in range(SLOTS):
                    rest(turn, s)
            for s in range(N_HB % SLOTS):
                rest(N_HB // SLOTS, s)

            for i in (2, 3):
                pool.wait_ge(ln_loaded[i], 16)
            for t in range(2):
                for half in range(2):
                    cols = slice(D // 2 * half, D // 2 * half + D // 2)
                    part = rows[:, t, cols]
                    if t == 0:
                        pool.wait_ge(row_normed, half + 1)
                        pool.tensor_tensor(part, part, ln_rows[:, 2, cols], ALU.mult).then_inc(pool_gained, 1)
                        pool.wait_ge(pool_gained, half + 1)
                    else:
                        pool.wait_ge(gained, half + 1)
                    pool.tensor_tensor(part, part, ln_rows[:, 3, cols], ALU.add).then_inc(out_made[t], 1)

        @block.scalar
        def _(act):

            def weights(n, turns=0):
                s = n % SLOTS
                act.wait_ge(raw_loaded[s % RAWS], 16 * (SLOTS // RAWS * turns + n // RAWS + 1))
                if n >= SLOTS:
                    act.wait_ge(w_used, SLOTS * turns + n - SLOTS + 1)
                act.activation(w_hi[:, s, :], raw[:, s % RAWS, :], ACT.Copy).then_inc(w_hi_made, 1)

            for k in range(KD):
                if k in (0, 3):
                    weights(k // 3)
                act.wait_ge(x_loaded[k // 2], 16)
                act.activation(act_hi[:, k, :], x_raw[:, k, :], ACT.Copy).then_inc(x_hi_made, 1)
            weights(2)
            act.dma_start(table[:, :], const).then_inc(table_loaded, 16)
            act.dma_start(gains[:, :], gain).then_inc(gains_loaded, 16)
            act.wait_ge(table_loaded, 16)
            act.activation(ident_r[:, :], ident, ACT.Copy)
            act.activation(mask_r[:, :], mask, ACT.Copy).then_inc(consts_made, 1)
            weights(3)

            def keep_latent(j):
                weights(2 * j + SLOTS)
                act.wait_ge(in_done, j + 1)
                if j == KL:
                    act.wait_ge(ssq_done, 1)
                act.activation(latent[:, j, :], bank[:, j % 2, :], ACT.Copy)
                act.activation(square[:, j % KL, :], bank[:, j % 2, :], ACT.Square).then_inc(latent_kept, 1)
                weights(2 * j + SLOTS + 1)

            def root_of(n, cols=slice(0, TT)):
                act.wait_ge(var_made, n + 1)
                act.activation(root[:, cols], ssq[:, cols], ACT.Sqrt).then_inc(root_made, 1)

            def latent_his(g):
                for j in range(KL * g, KL * g + KL):
                    act.wait_ge(latent_scaled, j + 1)
                    act.activation(mid_hi[:, j, :], latent[:, j, :], ACT.Copy).then_inc(latent_hi, 1)

            def rope_swap(r):
                act.wait_ge(rope_done, r + 1)
                if r is not KEY:
                    act.wait_ge(rope_rotated, r)
                for q in range(4):
                    last = act.activation(swap[32 * q:32 * q + 32, :],
                                          bank[32 * (q ^ 1):32 * (q ^ 1) + 32, 0 if r is KEY else 6, :], ACT.Copy)
                last.then_inc(rope_swapped, 1)

            KEY = 0
            for j in range(KL):
                keep_latent(j)
            for j in range(KL, 6):
                keep_latent(j)
            root_of(0)
            latent_his(0)
            keep_latent(6)
            keep_latent(7)
            root_of(1)
            weights(HB_QKV + 2)
            rope_swap(KEY)
            weights(HB_QKV + 3)
            latent_his(1)
            act.wait_ge(rope_rotated, 1)
            act.wait_ge(zeroed, 1)
            for h in range(2):
                half = slice(64 * h, 64 * h + 64)
                last = act.activation(kr_hi[half, h, :], rot[half, :], ACT.Copy)
            last.then_inc(rope_hi, 1)

            def proj_copy(pair, m, dst, b):
                act.wait_ge(proj_done, 6 * pair + m + 1)
                act.activation(dst, bank[:, b, :], ACT.Copy).then_inc(proj_hi, 1)

            def query(pair, h):
                proj_copy(pair, h, q_hi[:, h, :], 6 + h)

            def rope_query(pair):
                weights(HB_QKV + QKV_HB, pair)
                rope_swap(pair + 1)
                weights(HB_QKV + QKV_HB + 1, pair)

            def rope_query_hi(pair):
                act.wait_ge(rope_rotated, pair + 2)
                act.activation(qr_hi[:, :], rot[:, :], ACT.Copy).then_inc(rope_hi, 1)

            def key(pair, h):
                proj_copy(pair, 2 + h, k_hi[:, h, :], 7 - h)
                if h:
                    weights(HB_QKV + QKV_HB + 2, pair)

            def values(pair):
                for i in range(2):
                    proj_copy(pair, 4 + i, v_hi[:, 2 * i:2 * i + 2, :], 7 - i)
                weights(HB_QKV + QKV_HB + 3, pair)

            def exps(pair, h):
                act.wait_ge(max_negated, 2 * pair + h + 1)
                for t in range(TT):
                    at, n = SCORE_AT[t], P * (t + 1)
                    last = act.activation(probs[:, h, at:at + n], score_bank(h)[:, at:at + n], ACT.Exp,
                                          bias=neg_max[:, h, t:t + 1], scale=SCALE, accum_out=row_sum[:, h, t:t + 1])
                last.then_inc(exped, 1)

            def prob_t_his(pair, h):
                act.wait_ge(transposed, 2 * pair + h + 1)
                for a, b in ((0, 512), (512, SCORE_COLS)):
                    act.activation(pt_hi[:, h, a:b], score_bank(h)[:, a:b], ACT.Copy).then_inc(pt_hi_made, 1)

            def head_out_hi(pair, h):
                act.wait_ge(pv_done, 2 * pair + h + 1)
                act.activation(act_hi[:, bass.ds(2 * pair + h, 1), :].rearrange("p o s -> p (o s)"), bank[:, 3 * h, :],
                               ACT.Copy).then_inc(o_hi_made, 1)

            def attention(pair, ahead):
                exps(pair, 0)
                if ahead:
                    query(pair + 1, 0)
                exps(pair, 1)
                if ahead:
                    query(pair + 1, 1)
                    rope_query(pair + 1)
                prob_t_his(pair, 0)
                if ahead:
                    key(pair + 1, 0)
                    rope_query_hi(pair + 1)
                prob_t_his(pair, 1)
                if ahead:
                    key(pair + 1, 1)
                head_out_hi(pair, 0)
                head_out_hi(pair, 1)
                if ahead:
                    values(pair + 1)

            query(0, 0)
            query(0, 1)
            rope_query(0)
            rope_query_hi(0)
            key(0, 0)
            key(0, 1)
            values(0)
            with act.Fori(0, PAIRS - 1) as pair:
                attention(pair, True)
            attention(PAIRS - 1, False)

            act.wait_ge(o_split, HEADS)
            for t in range(TT):
                act.dma_start(rows[:, t, :], x[t]).then_inc(rows_loaded[t], 16)
            for i in range(4):
                act.dma_start(ln_rows[:, i, :], ln[i].partition_broadcast(P)).then_inc(ln_loaded[i], 16)

            with act.Fori(0, O_HB // SLOTS - 1) as turn:
                for s in range(SLOTS):
                    weights(HB_O + SLOTS + s, turn)
            for t in range(TT - 1):
                root_of(2 + t, slice(t, t + 1))
            weights(HB_MLP)
            weights(HB_MLP + 1)
            root_of(1 + TT, slice(TT - 1, TT))
            weights(HB_MLP + 2)

            for k in range(KD):
                act.wait_ge(t_done, k + 1)
                if k >= 2:
                    act.wait_ge(t_split, k - 1)
                act.activation(two[:, k % 2, :], bank[:, 4 + k % 2, :], ACT.Identity,
                               scale=gains[:, 8 + k:9 + k], bias=gains[:, 8 + KD + k:9 + KD + k]).then_inc(t_affine, 1)
                if k == 3:
                    weights(HB_MLP + SLOTS - 1)

            def hidden(c, j):
                act.wait_ge(up_done, CHUNK * c + j + 1)
                b = j % 2
                weights(HB_MLP + 2 * j + SLOTS, MLP_HB // SLOTS * c)
                if isinstance(c, int) and c == 0 and j < 2:
                    act.wait_ge(t_split, KD)
                else:
                    act.wait_ge(hid_squared, CHUNK * c + j - 1)
                act.activation(two[:, b, :], bank[:, 6 + b, :], ACT.Relu).then_inc(relu_made, 1)
                act.wait_ge(relu_made, CHUNK * c + j + 1)
                act.activation(mid_hi[:, j, :], two[:, b, :], ACT.Square).then_inc(hid_hi, 1)
                weights(HB_MLP + 2 * j + SLOTS + 1, MLP_HB // SLOTS * c)

            def chunk(c, last=False):
                for j in range(CHUNK):
                    hidden(c, j)
                for m in range(DOWN_HB - (SLOTS if last else 0)):
                    weights(HB_MLP + UP_HB + m + SLOTS, MLP_HB // SLOTS * c)

            chunk(0)
            with act.Fori(1, CHUNKS - 1) as c:
                chunk(c)
            chunk(CHUNKS - 1, last=True)
            for t in range(TT):
                root_of(2 + TT + t, slice(t, t + 1))
                act.wait_ge(row_scaled, TT + t + 1)
                for half in range(2):
                    part = rows[:, t, D // 2 * half:D // 2 * half + D // 2]
                    act.activation(part, part, ACT.Identity, scale=rstd[:, t:t + 1], bias=nmr[:, t:t + 1])\
                       .then_inc(row_normed, 1)

        @block.vector
        def _(dve):
            links = [0]

            def link(instruction):
                instruction.then_inc(dve_chain, 1)
                links[0] += 1
                dve.wait_ge(dve_chain, links[0])

            def inv_root(n, src, scale, eps, cols=slice(0, TT)):
                ssq, root, inv, tmp, rstd = (v[:, cols] for v in all_roots)
                dve.tensor_scalar(ssq, src, scale, eps, ALU.mult, ALU.add).then_inc(var_made, 1)
                dve.wait_ge(root_made, n + 1)
                link(dve.reciprocal(inv, root))
                link(dve.tensor_tensor(tmp, inv, inv, ALU.mult))
                link(dve.tensor_tensor(tmp, tmp, ssq, ALU.mult))
                link(dve.tensor_scalar(tmp, tmp, -0.5, 1.5, ALU.mult, ALU.add))
                link(dve.tensor_tensor(rstd, inv, tmp, ALU.mult))

            dve.memset(ones[:, :], 1.0).then_inc(consts_made, 1)
            for k in range(KD):
                dve.wait_ge(x_hi_made, k + 1)
                dve.tensor_tensor(act_lo[:, k, :], x_raw[:, k, :], act_hi[:, k, :].bitcast(f32), ALU.subtract)\
                   .then_inc(x_split, 1)
            dve.wait_ge(x_split, KD)
            for part in (kr_hi, kr_lo):
                for h in range(2):
                    last = dve.memset(part[64 - 64 * h:128 - 64 * h, h, :].bitcast(f32), 0.0)
            last.then_inc(zeroed, 1)

            def scale_latent(g):
                dve.wait_ge(ssq_done, g + 1)
                if g:
                    dve.wait_ge(inv_spread, g)
                inv_root(g, bank[:, 2, TT * g:TT * g + TT], 1.0 / LORA, RMS_EPS)
                for t in range(TT):
                    last = dve.tensor_scalar(diag[:, t, :], ident, rstd[:, t:t + 1], None, ALU.mult)
                last.then_inc(diag_made, 1)
                dve.wait_ge(inv_spread, g + 1)
                for j in range(KL * g, KL * g + KL):
                    dve.scalar_tensor_tensor(out=latent[:, j, :], in0=latent[:, j, :], scalar=gains[:, j:j + 1],
                                             in1=bank[:, 3, :], op0=ALU.mult, op1=ALU.mult).then_inc(latent_scaled, 1)

            def latent_los(g):
                for j in range(KL * g, KL * g + KL):
                    dve.wait_ge(latent_hi, j + 1)
                    dve.tensor_tensor(mid_lo[:, j, :], latent[:, j, :], mid_hi[:, j, :].bitcast(f32), ALU.subtract)\
                       .then_inc(latent_split, 1)

            KEY = 0

            def rotate(r, b):
                dve.wait_ge(rope_swapped, r + 1)
                if r is not KEY:
                    dve.wait_ge(rope_split, r)
                dve.tensor_tensor(rot[:, :], bank[:, b, :], rope_cos, ALU.mult).then_inc(rope_cosined, 1)
                dve.tensor_tensor(swap[:, :], swap[:, :], rope_sin, ALU.mult).then_inc(rope_sined, 1)
                dve.wait_ge(rope_cosined, r + 1)
                dve.wait_ge(rope_sined, r + 1)
                dve.tensor_tensor(rot[:, :], rot[:, :], swap[:, :], ALU.add).then_inc(rope_rotated, 1)

            dve.wait_ge(gains_loaded, 16)
            scale_latent(0)
            latent_los(0)
            scale_latent(1)
            rotate(KEY, 0)
            latent_los(1)
            dve.wait_ge(rope_hi, 1)
            for h in range(2):
                half = slice(64 * h, 64 * h + 64)
                last = dve.tensor_tensor(kr_lo[half, h, :], rot[half, :], kr_hi[half, h, :].bitcast(f32), ALU.subtract)
            last.then_inc(rope_split, 1)

            def proj_rest(pair, m, lo, hi, b):
                dve.wait_ge(proj_hi, 6 * pair + m + 1)
                dve.tensor_tensor(lo, bank[:, b, :], hi.bitcast(f32), ALU.subtract).then_inc(proj_split, 1)

            def query(pair, h):
                proj_rest(pair, h, q_lo[:, h, :], q_hi[:, h, :], 6 + h)

            def rope_query(pair):
                rotate(pair + 1, 6)

            def rope_query_lo(pair):
                dve.wait_ge(rope_hi, pair + 2)
                dve.tensor_tensor(qr_lo[:, :], rot[:, :], qr_hi[:, :].bitcast(f32), ALU.subtract).then_inc(rope_split, 1)

            def key(pair, h):
                proj_rest(pair, 2 + h, k_lo[:, h, :], k_hi[:, h, :], 7 - h)

            def values(pair):
                for i in range(2):
                    part = slice(2 * i, 2 * i + 2)
                    proj_rest(pair, 4 + i, v_lo[:, part, :].rearrange("p t d -> p (t d)"),
                              v_hi[:, part, :].rearrange("p t d -> p (t d)"), 7 - i)

            def maxima(pair, h):
                dve.wait_ge(scored, 2 * pair + h + 1)
                for t in range(TT):
                    at, n = SCORE_AT[t], P * (t + 1)
                    last = dve.reduce_max(row_max[:, h, t:t + 1], score_bank(h)[:, at:at + n], AX.X)
                last.then_inc(maxed, 1)
                dve.wait_ge(maxed, 2 * pair + h + 1)
                dve.tensor_scalar(neg_max[:, h, :], row_max[:, h, :], -SCALE, None, ALU.mult).then_inc(max_negated, 1)

            def normalise(pair, h):
                dve.wait_ge(exped, 2 * pair + h + 1)
                dve.reciprocal(inv_sum[:, h, :], row_sum[:, h, :]).then_inc(sum_inverted, 1)
                dve.wait_ge(sum_inverted, 2 * pair + h + 1)
                for t in range(TT):
                    at, n = SCORE_AT[t], P * (t + 1)
                    last = dve.tensor_scalar(probs[:, h, at:at + n], probs[:, h, at:at + n], inv_sum[:, h, t:t + 1],
                                             None, ALU.mult)
                last.then_inc(normed, 1)

            def prob_t_los(pair, h):
                for i, (a, b) in enumerate(((0, 512), (512, SCORE_COLS))):
                    dve.wait_ge(pt_hi_made, 4 * pair + 2 * h + i + 1)
                    dve.tensor_tensor(pt_lo[:, h, a:b], score_bank(h)[:, a:b], pt_hi[:, h, a:b].bitcast(f32),
                                      ALU.subtract).then_inc(pt_split, 1)

            def head_out_lo(pair, h):
                dve.wait_ge(o_hi_made, 2 * pair + h + 1)
                head = bass.ds(2 * pair + h, 1)
                dve.tensor_tensor(act_lo[:, head, :].rearrange("p o s -> p (o s)"), bank[:, 3 * h, :],
                                  act_hi[:, head, :].rearrange("p o s -> p (o s)").bitcast(f32), ALU.subtract)\
                   .then_inc(o_split, 1)

            def attention(pair, ahead):
                maxima(pair, 0)
                maxima(pair, 1)
                normalise(pair, 0)
                if ahead:
                    query(pair + 1, 0)
                normalise(pair, 1)
                if ahead:
                    query(pair + 1, 1)
                    rope_query(pair + 1)
                prob_t_los(pair, 0)
                if ahead:
                    key(pair + 1, 0)
                    rope_query_lo(pair + 1)
                prob_t_los(pair, 1)
                if ahead:
                    key(pair + 1, 1)
                head_out_lo(pair, 0)
                head_out_lo(pair, 1)
                if ahead:
                    values(pair + 1)

            query(0, 0)
            query(0, 1)
            rope_query(0)
            rope_query_lo(0)
            key(0, 0)
            key(0, 1)
            values(0)
            with dve.Fori(0, PAIRS - 1) as pair:
                attention(pair, True)
            attention(PAIRS - 1, False)

            def row_bank(cg, t):
                return bank[:, t + (4 if cg % 2 == 0 else 0), :]

            def add_row_part(rnd, cg, t):
                dve.wait_ge(block_done, 16 * rnd + 4 * cg + t + 1)
                part = rows[:, t, 512 * cg:512 * cg + 512]
                scale = ALPHA if isinstance(rnd, int) and rnd == 0 else 1.0
                dve.scalar_tensor_tensor(out=part, in0=part, scalar=scale, in1=row_bank(cg, t), op0=ALU.mult,
                                         op1=ALU.add).then_inc(rows_added, 1)

            def measure_part(rnd, cg, t):
                dve.wait_ge(rows_added, 16 * rnd + 4 * cg + t + 1)
                dve.bn_stats(stats[:, t, cg, :], rows[:, t, 512 * cg:512 * cg + 512]).then_inc(row_stats, 1)

            def add_rows(rnd, cg):
                for t in range(TT):
                    add_row_part(rnd, cg, t)

            def measure(rnd, cg):
                for t in range(TT):
                    measure_part(rnd, cg, t)

            def aggregate(n, t):
                dve.wait_ge(row_stats, 16 * n + 12 + t + 1)
                one = slice(t, t + 1)
                link(dve.bn_aggr(moments[:, t, :], stats[:, t, :, :].rearrange("p c s -> p (c s)")))
                inv_root(2 + TT * n + t, moments[:, t, 1:2], 1.0, LN_EPS, one)
                link(dve.tensor_tensor(tmp[:, one], moments[:, t, 0:1], rstd[:, one], ALU.mult))
                dve.tensor_scalar(nmr[:, one], tmp[:, one], -1.0, None, ALU.mult).then_inc(row_scaled, 1)

            for t in range(TT):
                dve.wait_ge(rows_loaded[t], 16)
            for cg in range(CG - 1):
                add_rows(0, cg)
                measure(0, cg)
            for t in range(TT):
                add_row_part(0, CG - 1, t)
                measure_part(0, CG - 1, t)
                aggregate(0, t)
                dve.wait_ge(row_scaled, t + 1)
                pieces = 1 if t < TT - 1 else CG
                for i in range(pieces):
                    part = rows[:, t, D // pieces * i:D // pieces * (i + 1)]
                    dve.tensor_scalar(part, part, rstd[:, t:t + 1], nmr[:, t:t + 1], ALU.mult, ALU.add).then_inc(normed, 1)
            for k in range(KD):
                dve.wait_ge(t_affine, k + 1)
                dve.tensor_copy(act_hi[:, k, :], two[:, k % 2, :]).then_inc(t_hi, 1)
                dve.wait_ge(t_hi, k + 1)
                dve.tensor_tensor(act_lo[:, k, :], two[:, k % 2, :], act_hi[:, k, :].bitcast(f32), ALU.subtract)\
                   .then_inc(t_split, 1)

            def hidden(c, j):
                b = bank[:, 6 + j % 2, :]
                dve.wait_ge(relu_made, CHUNK * c + j + 1)
                dve.scalar_tensor_tensor(out=b, in0=b, scalar=0.0, in1=two[:, j % 2, :], op0=ALU.max, op1=ALU.mult)\
                   .then_inc(hid_squared, 1)
                dve.wait_ge(hid_squared, CHUNK * c + j + 1)
                dve.wait_ge(hid_hi, CHUNK * c + j + 1)
                dve.tensor_tensor(mid_lo[:, j, :], b, mid_hi[:, j, :].bitcast(f32), ALU.subtract).then_inc(hid_split, 1)

            def residual(i):
                t, half = i // 2, slice(1024 * (i % 2), 1024 * (i % 2) + 1024)
                part = rows[:, t, half]
                dve.scalar_tensor_tensor(out=part, in0=part, scalar=ALPHA, in1=ln_rows[:, 0, half], op0=ALU.mult,
                                         op1=ALU.mult).then_inc(residual_scaled, 1)
                dve.wait_ge(residual_scaled, i + 1)
                dve.scalar_tensor_tensor(out=part, in0=ln_rows[:, 1, half], scalar=ALPHA, in1=part, op0=ALU.mult,
                                         op1=ALU.add).then_inc(residual_made, 1)

            dve.wait_ge(ln_loaded[0], 16)
            dve.wait_ge(ln_loaded[1], 16)
            dve.wait_ge(t_done, KD)
            for j in range(CHUNK):
                hidden(0, j)
                residual(j)
            dve.wait_ge(residual_made, 8)
            for cg in range(CG):
                add_rows(1, cg)
            with dve.Fori(1, CHUNKS - 1) as c:
                for j in range(CHUNK):
                    hidden(c, j)
                for cg in range(CG):
                    add_rows(c + 1, cg)
            for j in range(CHUNK):
                hidden(CHUNKS - 1, j)
            for cg in range(CG - 1):
                add_rows(CHUNKS, cg)
                measure(CHUNKS, cg)
            for i in (2, 3):
                dve.wait_ge(ln_loaded[i], 16)
            for t in range(TT):
                add_row_part(CHUNKS, CG - 1, t)
                measure_part(CHUNKS, CG - 1, t)
                aggregate(1, t)
                for half in range(2 if t else 0):
                    cols = slice(D // 2 * half, D // 2 * half + D // 2)
                    part = rows[:, t, cols]
                    dve.wait_ge(row_normed, 2 * t + half + 1)
                    dve.tensor_tensor(part, part, ln_rows[:, 2, cols], ALU.mult).then_inc(gained, 1)
                    if t > 1:
                        dve.wait_ge(gained, 2 * (t - 1) + half + 1)
                        dve.tensor_tensor(part, part, ln_rows[:, 3, cols], ALU.add).then_inc(out_made[t], 1)

        @block.tensor
        def _(pe):
            read_out = [0]

            def weights_read():
                read_out[0] += 1

            def product(out_, a_hi, a_lo, b_hi, b_lo, start, stop):
                first_pass = pe.matmul(out_, a_hi, b_hi, start=start, stop=False)
                if read_out[0]:
                    first_pass.then_inc(w_used, read_out[0])
                    read_out[0] = 0
                pe.matmul(out_, a_hi, b_lo, start=False, stop=False)
                return pe.matmul(out_, a_lo, b_hi, start=False, stop=stop)

            def stream_tile(n, slot, dst, ready=None):
                for half in range(2):
                    s = (slot + half) % SLOTS
                    pe.wait_ge(w_split, n + half + 1)
                    for kk in range(KD // 2):
                        k = half * KD // 2 + kk
                        if ready:
                            ready(k)
                        cols = slice(P * kk, P * kk + P)
                        last = product(dst, w_hi[:, s, cols], w_lo[:, s, cols], act_hi[:, k, :], act_lo[:, k, :],
                                       k == 0, k == KD - 1)
                    weights_read()
                return last

            def in_tile(j, b):
                if not (isinstance(j, int) and j < 2):
                    pe.wait_ge(latent_kept, j - 1)
                last = stream_tile(2 * j, 2 * b, bank[:, b, :])
                return last

            def sum_squares(g):
                pe.wait_ge(latent_kept, KL * g + KL)
                for t in range(TT):
                    for j in range(KL):
                        last = pe.matmul(bank[:, 2, TT * g + t:TT * g + t + 1], square[:, j, P * t:P * t + P], ones[:, 0:1],
                                         start=j == 0, stop=j == KL - 1)
                last.then_inc(ssq_done, 1)

            def spread_inverse(g):
                pe.wait_ge(diag_made, g + 1)
                if g:
                    pe.wait_ge(latent_scaled, KL)
                for t in range(TT):
                    last = pe.matmul(bank[:, 3, P * t:P * t + P], ones[:, :], diag[:, t, :], start=True, stop=True)
                last.then_inc(inv_spread, 1)

            for j in range(2):
                def x_ready(k, j=j):
                    if j == 0:
                        pe.wait_ge(x_split, k + 1)
                last = stream_tile(2 * j, 2 * j, bank[:, j, :], x_ready)
                last.then_inc(in_done, 1)
            with pe.Fori(1, 3) as i:
                for b in range(2):
                    in_tile(2 * i + b, b).then_inc(in_done, 1)
            pe.wait_ge(consts_made, 2)
            sum_squares(0)
            in_tile(6, 0).then_inc(in_done, 1)
            spread_inverse(0)
            in_tile(7, 1).then_inc(in_done, 1)
            pe.wait_ge(latent_kept, 7)

            def squares_midway(k):
                if k == 5:
                    sum_squares(1)
            stream_tile(16, 0, bank[:, 0, :], squares_midway).then_inc(rope_done, 1)

            def head_tile(pair, hb, at, lat, dst, width=P):
                s = (HB_QKV + hb) % SLOTS
                pe.wait_ge(w_split, HB_QKV + QKV_HB * pair + hb + 1)
                for k in range(KL):
                    cols = slice(at + width * k, at + width * k + P)
                    last = product(dst, w_hi[:, s, cols], w_lo[:, s, cols], mid_hi[:, lat + k, :], mid_lo[:, lat + k, :],
                                   k == 0, k == KL - 1)
                return last

            def first(pair):
                return isinstance(pair, int) and pair == 0

            def query(pair, h):
                if first(pair):
                    pe.wait_ge(latent_split, KL)
                else:
                    pe.wait_ge(proj_split, 6 * pair - h)
                last = head_tile(pair, 0, KL * P * h, 0, bank[:, 6 + h, :])
                last.then_inc(proj_done, 1)
                if h:
                    weights_read()

            def rope_query(pair):
                pe.wait_ge(proj_split, 6 * pair + 1)
                head_tile(pair, 1, 0, 0, bank[:, 6, :]).then_inc(rope_done, 1)
                weights_read()

            def key(pair, h):
                if h == 0:
                    if first(pair):
                        pe.wait_ge(latent_split, 2 * KL)
                    pe.wait_ge(proj_split, 6 * pair + 2)
                else:
                    pe.wait_ge(rope_rotated, pair + 2)
                head_tile(pair, 2, KL * P * h, KL, bank[:, 7 - h, :]).then_inc(proj_done, 1)
                if h:
                    weights_read()

            def value(pair, i):
                s = (HB_QKV + 3) % SLOTS
                pe.wait_ge(w_split, HB_QKV + QKV_HB * pair + 4)
                pe.wait_ge(proj_split, 6 * pair + 3 + i)
                for half in range(2):
                    tok = slice(P * (2 * i + half), P * (2 * i + half) + P)
                    for k in range(KL):
                        cols = slice(2 * VDIM * k, 2 * VDIM * k + 2 * VDIM)
                        last = product(bank[:, 7 - i, 256 * half:256 * half + 256], mid_hi[:, KL + k, tok],
                                       mid_lo[:, KL + k, tok], w_hi[:, s, cols], w_lo[:, s, cols], k == 0, k == KL - 1)
                last.then_inc(proj_done, 1)
                if i:
                    weights_read()

            def scores(pair, h):
                if h == 0:
                    pe.wait_ge(proj_split, 6 * pair + 4)
                    pe.wait_ge(rope_split, pair + 2)
                if not first(pair):
                    pe.wait_ge(o_split, 2 * pair + h - 1)
                for t in range(TT):
                    q, keys = slice(P * t, P * t + P), slice(0, P * (t + 1))
                    dst = score_bank(h)[:, SCORE_AT[t]:SCORE_AT[t] + P * (t + 1)]
                    product(dst, q_hi[:, h, q], q_lo[:, h, q], k_hi[:, h, keys], k_lo[:, h, keys], True, False)
                    product(dst, qr_hi[:, q], qr_lo[:, q], kr_hi[:, h, keys], kr_lo[:, h, keys], False, False)
                    last = pe.matmul(dst[:, P * t:P * t + P], ident_r[:, :], mask_r[:, :], start=False, stop=True)
                last.then_inc(scored, 1)

            def transpose_probs(pair, h):
                pe.wait_ge(normed, 2 * pair + h + 1)
                for k in range(TT):
                    for t in range(k, TT):
                        at = PROB_T_AT[k] + P * (t - k)
                        last = pe.transpose(score_bank(h)[:, at:at + P],
                                            probs[:, h, SCORE_AT[t] + P * k:SCORE_AT[t] + P * k + P], ident)
                last.then_inc(transposed, 1)

            def weigh_values(pair, h):
                if h == 0:
                    pe.wait_ge(proj_split, 6 * pair + 6)
                pe.wait_ge(pt_split, 4 * pair + 2 * h + 2)
                for k in range(TT):
                    at, n = PROB_T_AT[k], S - P * k
                    v = slice(VDIM * h, VDIM * h + VDIM)
                    last = product(bank[:, 3 * h, P * k:S], v_hi[:, k, v], v_lo[:, k, v], pt_hi[:, h, at:at + n],
                                   pt_lo[:, h, at:at + n], k == 0, k == TT - 1)
                last.then_inc(pv_done, 1)

            def attention(pair, ahead):
                scores(pair, 0)
                scores(pair, 1)
                if ahead:
                    query(pair + 1, 0)
                    query(pair + 1, 1)
                    rope_query(pair + 1)
                transpose_probs(pair, 0)
                if ahead:
                    key(pair + 1, 0)
                transpose_probs(pair, 1)
                if ahead:
                    key(pair + 1, 1)
                    value(pair + 1, 0)
                weigh_values(pair, 0)
                weigh_values(pair, 1)
                if ahead:
                    value(pair + 1, 1)

            spread_inverse(1)
            query(0, 0)
            query(0, 1)
            rope_query(0)
            key(0, 0)
            key(0, 1)
            value(0, 0)
            value(0, 1)
            attention(0, True)
            with pe.Fori(1, PAIRS - 1) as pair:
                attention(pair, True)
            attention(PAIRS - 1, False)

            def row_part(rnd, cg, parity, m, t, src_hi, src_lo, last_m):
                s = (HB_O + m) % SLOTS
                dst = bank[:, t + (0 if parity else 4), :]
                if m == 0 and not (isinstance(rnd, int) and rnd == 0 and cg < 2):
                    if parity == 0 and isinstance(cg, int) and cg == 0:
                        if t >= 2:
                            pe.wait_ge(hid_split, CHUNK * (rnd - 1) + 5 + t)
                    else:
                        pe.wait_ge(rows_added, 16 * rnd + 4 * cg - 8 + t + 1)
                for kk in range(2):
                    k = 2 * m + kk
                    tok = slice(P * t, P * t + P)
                    cols = slice(512 * kk, 512 * kk + 512)
                    last = product(dst, src_hi[:, k, tok], src_lo[:, k, tok], w_hi[:, s, cols], w_lo[:, s, cols],
                                   k == 0, m == last_m and kk == 1)
                if m == last_m:
                    last.then_inc(block_done, 1)

            def row_block(rnd, cg, parity, m, n, src_hi, src_lo, last_m):
                pe.wait_ge(w_split, n + 1)
                for t in range(TT):
                    row_part(rnd, cg, parity, m, t, src_hi, src_lo, last_m)
                weights_read()

            def row_blocks_by_token(rnd, n, src_hi, src_lo, last_m):
                for t in range(TT):
                    for i in range(SLOTS):
                        if t == 0:
                            pe.wait_ge(w_split, n + i + 1)
                        row_part(rnd, CG - 1, 1, last_m - SLOTS + 1 + i, t, src_hi, src_lo, last_m)
                        if t == TT - 1:
                            weights_read()

            for cg in range(CG):
                for m in range(KD // 2 - (SLOTS if cg == CG - 1 else 0)):
                    if cg == 0 and m == KD // 2 - 1:
                        pe.wait_ge(o_split, HEADS)
                    row_block(0, cg, cg % 2, m, HB_O + KD // 2 * cg + m, act_hi, act_lo, KD // 2 - 1)

            row_blocks_by_token(0, HB_MLP - SLOTS, act_hi, act_lo, KD // 2 - 1)

            def transpose_rows(k):
                if k % 4 == 0:
                    pe.wait_ge(normed, HEADS + TT + k // 4)
                if k >= 2:
                    pe.wait_ge(t_split, k - 1)
                for t in range(TT):
                    last = pe.transpose(bank[:, 4 + k % 2, P * t:P * t + P], rows[:, t, P * k:P * k + P], ident)
                last.then_inc(t_done, 1)

            def up_tile(c, j, b, ready=None):
                if isinstance(j, int) and j < 2:
                    pe.wait_ge(rows_added, 16 * c + 12)
                else:
                    pe.wait_ge(hid_split, CHUNK * c + j - 1)
                n = HB_MLP + MLP_HB * c + 2 * j
                stream_tile(n, (HB_MLP + 2 * b) % SLOTS, bank[:, 6 + b, :], ready).then_inc(up_done, 1)

            def down(c, last=False):
                n = HB_MLP + MLP_HB * c + UP_HB
                for cg in range(CG - 1 if last else CG):
                    for m in range(CHUNK // 2):
                        if cg == 0:
                            pe.wait_ge(hid_split, CHUNK * c + 2 * m + 2)
                        row_block(c + 1, cg, cg % 2, m, n + CHUNK // 2 * cg + m, mid_hi, mid_lo, CHUNK // 2 - 1)
                if last:
                    row_blocks_by_token(c + 1, N_HB - SLOTS, mid_hi, mid_lo, CHUNK // 2 - 1)

            def first_ready(k):
                if k == 0:
                    transpose_rows(0)
                    transpose_rows(1)
                if k + 2 < KD:
                    transpose_rows(k + 2)
                pe.wait_ge(t_split, k + 1)

            up_tile(0, 0, 0, first_ready)
            up_tile(0, 1, 1)
            with pe.Fori(1, CHUNK // 2) as i:
                for b in range(2):
                    up_tile(0, 2 * i + b, b)
            down(0)

            def up(c):
                for b in range(2):
                    up_tile(c, b, b)
                with pe.Fori(1, CHUNK // 2) as i:
                    for b in range(2):
                        up_tile(c, 2 * i + b, b)

            with pe.Fori(1, CHUNKS - 1) as c:
                up(c)
                down(c)
            up(CHUNKS - 1)
            down(CHUNKS - 1, last=True)


def _stream(w_in, w_uq, w_ukv, w_o, w1, w2):
    import numpy as np
    out = np.zeros((N_HB, P, HB), np.float32)
    w_in = np.concatenate([w_in[:, :2 * LORA], w_in[:, 2 * LORA:], w_in[:, 2 * LORA:]], axis=1)
    out[:IN_HB] = w_in.reshape(2, KD // 2, P, IN_TILES, P).transpose(3, 0, 2, 1, 4).reshape(IN_HB, P, HB)
    qkv = out[HB_QKV:HB_O].reshape(PAIRS, QKV_HB, P, HB)
    uq = w_uq.reshape(KL, P, PAIRS, 2, NOPE + ROPE)
    qkv[:, 0] = uq[..., :NOPE].transpose(2, 1, 3, 0, 4).reshape(PAIRS, P, HB)
    qkv[:, 1, :, :HB // 2] = uq[..., NOPE:].transpose(2, 1, 0, 3, 4).reshape(PAIRS, P, HB // 2)
    ukv = w_ukv.reshape(KL, P, PAIRS, 2, NOPE + VDIM)
    qkv[:, 2] = ukv[..., :NOPE].transpose(2, 1, 3, 0, 4).reshape(PAIRS, P, HB)
    qkv[:, 3] = ukv[..., NOPE:].transpose(2, 1, 0, 3, 4).reshape(PAIRS, P, HB)
    out[HB_O:HB_MLP] = w_o.reshape(KD // 2, 2, P, CG, 512).transpose(3, 0, 2, 1, 4).reshape(O_HB, P, HB)
    mlp = out[HB_MLP:].reshape(CHUNKS, MLP_HB, P, HB)
    mlp[:, :UP_HB] = w1.reshape(2, KD // 2, P, CHUNKS, CHUNK, P).transpose(3, 4, 0, 2, 1, 5)\
        .reshape(CHUNKS, UP_HB, P, HB)
    mlp[:, UP_HB:] = w2.reshape(CHUNKS, CHUNK // 2, 2, P, CG, 512).transpose(0, 4, 1, 3, 2, 5)\
        .reshape(CHUNKS, DOWN_HB, P, HB)
    return out


def _tables():
    import numpy as np
    inv = (1.0 / (np.float32(10000.0) ** (np.arange(0, ROPE, 2, dtype=np.float32) / np.float32(ROPE)))).astype(np.float32)
    ang = inv[:, None] * np.arange(S, dtype=np.float32)[None, :]
    cos, sin = np.cos(ang).astype(np.float32), np.sin(ang).astype(np.float32)
    ident = np.eye(P, dtype=np.float32)
    mask = np.where(np.arange(P)[None, :] <= np.arange(P)[:, None], 0.0, MASKED).astype(np.float32)
    return np.ascontiguousarray(np.concatenate(
        [ident, mask, np.concatenate([cos] * 4), np.concatenate([-sin, sin] * 2)], axis=1))


def kernel(x, mla_w_in, mla_q_norm, mla_kv_norm, mla_w_uq, mla_w_ukv, mla_w_o,
           hgrn_w_in, hgrn_lb_logits, hgrn_o_norm, hgrn_w_o, sb_w_in, sb_w_o, moba_w_in, moba_w_o,
           ln_g, ln_b, mlp_w1, mlp_w2):
    import numpy as np
    import concourse.bacc as _bacc
    from concourse.bass_utils import run_bass_kernel_spmd as _run

    x = np.asarray(x)[0]
    arrays = {
        "x_t": np.ascontiguousarray(x.T.reshape(KD, P, S).transpose(1, 0, 2)),
        "x_rows": np.ascontiguousarray(x.reshape(TT, P, D)),
        "weights": _stream(*(np.asarray(a)[0] for a in (mla_w_in, mla_w_uq, mla_w_ukv, mla_w_o, mlp_w1, mlp_w2))),
        "tables": _tables(),
        "gains": np.ascontiguousarray(np.concatenate(
            [np.asarray(a).reshape(-1, P).T for a in (mla_q_norm[0], mla_kv_norm[0], ln_g[0, 0], ln_b[0, 0])], axis=1)),
        "ln": np.ascontiguousarray(np.stack([np.asarray(a) for a in (ln_g[0, 0], ln_b[0, 0], ln_g[0, 1], ln_b[0, 1])])),
    }
    nc = _bacc.Bacc("TRN2", target_bir_lowering=False, num_devices=1)
    args = [nc.dram_tensor(name, a.shape, mybir.dt.float32, kind="ExternalInput").ap() for name, a in arrays.items()]
    out = nc.dram_tensor("out_rows", (TT, P, D), mybir.dt.float32, kind="ExternalOutput").ap()
    mla_mlp_program(nc, *args, out)
    r = _run(nc, [arrays], core_ids=[0])
    return r.results[0]["out_rows"].reshape(1, S, D)
```
